# Optimizing a Trainium2 kernel written in Bass

```python
import math
import jax, jax.numpy as jnp
from jax import lax
import numpy as np

D_MODEL = 1024
BATCH = 1
SEQ = 512
DEPTH = 2

N_MIXERS = 2
N_RET_LAYERS = (DEPTH + 1) // 2
N_DSA_LAYERS = DEPTH // 2
D_FF = 2816
RMS_EPS = 1e-6

RET_HEADS = 4
RET_DK = D_MODEL // RET_HEADS
RET_DV = 2 * RET_DK
RET_CHUNK = 128
ROT_BASE = 10000.0
RET_IN = 2 * RET_HEADS * RET_DK + 2 * RET_HEADS * RET_DV

DSA_HEADS = 8
DSA_HEAD_DIM = D_MODEL // DSA_HEADS
DSA_Q_RANK = 256
DSA_KV_RANK = 256
IDX_HEADS = 8
IDX_DIM = 64
TOPK_MAX = 256
Q_BLOCK = 128
DSA_IN = DSA_Q_RANK + DSA_KV_RANK + IDX_DIM + IDX_HEADS

kernel_name = 'hybrid_retention_dsa_macaron'

def rmsnorm(x, g):
    xf = x.astype(jnp.float32)
    y = xf * lax.rsqrt(jnp.mean(xf * xf, axis=-1, keepdims=True) + RMS_EPS)
    return (y * g.astype(jnp.float32)).astype(x.dtype)

def layernorm(x, g, b):
    xf = x.astype(jnp.float32)
    mu = jnp.mean(xf, axis=-1, keepdims=True)
    var = jnp.mean(jnp.square(xf - mu), axis=-1, keepdims=True)
    y = (xf - mu) * lax.rsqrt(var + RMS_EPS)
    return (y * g.astype(jnp.float32) + b.astype(jnp.float32)).astype(x.dtype)

def swiglu(h, w_in, w_out):
    gate, up = jnp.split(h @ w_in, 2, axis=-1)
    return (jax.nn.silu(gate) * up) @ w_out

def rotate_pairs(t, cos, sin):
    tp = t.astype(jnp.float32).reshape(t.shape[:-1] + (t.shape[-1] // 2, 2))
    t0, t1 = tp[..., 0], tp[..., 1]
    c = cos[None, :, None, :]
    s = sin[None, :, None, :]
    out = jnp.stack([t0 * c - t1 * s, t1 * c + t0 * s], axis=-1)
    return out.reshape(t.shape).astype(t.dtype)

def retention(h, w_in, w_out):
    B, S, _ = h.shape
    H, dk, dv, C = RET_HEADS, RET_DK, RET_DV, RET_CHUNK
    n_chunks = S // C
    q, k, v, g = jnp.split(h @ w_in, [H * dk, 2 * H * dk, 2 * H * dk + H * dv], axis=-1)
    q = q.reshape(B, S, H, dk)
    k = k.reshape(B, S, H, dk)
    v = v.reshape(B, S, H, dv)
    pos = jnp.arange(S, dtype=jnp.float32)
    freq = 1.0 / (ROT_BASE ** jnp.linspace(0.0, 1.0, dk // 2, dtype=jnp.float32))
    ang = pos[:, None] * freq[None, :]
    cos, sin = jnp.cos(ang), jnp.sin(ang)
    q = rotate_pairs(q, cos, sin)
    k = rotate_pairs(k, cos, sin) * (dk ** -0.5)
    log_gamma = jnp.log(1.0 - 2.0 ** (-5.0 - jnp.arange(H, dtype=jnp.float32)))
    idx = jnp.arange(C, dtype=jnp.float32)
    diff = idx[:, None] - idx[None, :]
    inner_decay = jnp.where(diff[None] >= 0, jnp.exp(jnp.maximum(diff, 0.0)[None] * log_gamma[:, None, None]), 0.0)
    q_decay = jnp.exp((idx[None, :] + 1.0) * log_gamma[:, None])
    k_decay = jnp.exp((C - 1.0 - idx[None, :]) * log_gamma[:, None])
    chunk_decay = jnp.exp(C * log_gamma)

    def to_chunks(t):
        return t.reshape(B, n_chunks, C, H, t.shape[-1]).transpose(1, 0, 3, 2, 4)

    def step(state, inp):
        qc, kc, vc = inp
        scores = jnp.einsum('bhid,bhjd->bhij', qc, kc) * inner_decay[None]
        inner = jnp.einsum('bhij,bhje->bhie', scores, vc)
        cross = jnp.einsum('bhid,bhde->bhie', qc, state) * q_decay[None, :, :, None]
        new_state = state * chunk_decay[None, :, None, None] + jnp.einsum(
            'bhjd,bhje->bhde', kc * k_decay[None, :, :, None], vc)
        return new_state, inner + cross

    state0 = jnp.zeros((B, H, dk, dv), jnp.float32)
    _, out = lax.scan(step, state0, (to_chunks(q), to_chunks(k), to_chunks(v)))
    out = out.transpose(1, 0, 3, 2, 4).reshape(B, S, H, dv).astype(jnp.float32)
    out = out * lax.rsqrt(jnp.mean(out * out, axis=-1, keepdims=True) + RMS_EPS)
    out = out.reshape(B, S, H * dv).astype(h.dtype)
    return (jax.nn.silu(g) * out) @ w_out

def dsa_attention(h, w_in, q_norm, kv_norm, w_uq, w_qidx, kidx_g, kidx_b, w_uk, w_uv, w_out):
    B, S, _ = h.shape
    H, dh, HI, DI = DSA_HEADS, DSA_HEAD_DIM, IDX_HEADS, IDX_DIM
    n_blocks = S // Q_BLOCK
    top_k = min(TOPK_MAX, S // 4)
    c_q, c_kv, k_idx, w_idx = jnp.split(
        h @ w_in, [DSA_Q_RANK, DSA_Q_RANK + DSA_KV_RANK, DSA_Q_RANK + DSA_KV_RANK + IDX_DIM], axis=-1)
    c_q = rmsnorm(c_q, q_norm)
    c_kv = rmsnorm(c_kv, kv_norm)
    k_idx = layernorm(k_idx, kidx_g, kidx_b)
    w_idx = w_idx * (HI ** -0.5)
    key_pos = jnp.arange(S)
    batch_ix = jnp.arange(B)[:, None, None]

    def block(args):
        blk, cq_b, w_b = args
        q_pos = blk * Q_BLOCK + jnp.arange(Q_BLOCK)
        q_idx = (cq_b @ w_qidx).reshape(B, Q_BLOCK, HI, DI)
        dots = jnp.einsum('bthd,bsd->btsh', q_idx, k_idx) * (DI ** -0.5)
        score = jnp.einsum('btsh,bth->bts', jax.nn.relu(dots), w_b).astype(jnp.float32)
        causal = key_pos[None, :] <= q_pos[:, None]
        score = jnp.where(causal[None], score, -jnp.inf)
        _, sel = lax.top_k(score, top_k)
        valid = sel <= q_pos[None, :, None]
        c_sel = c_kv[batch_ix, sel]
        q = (cq_b @ w_uq).reshape(B, Q_BLOCK, H, dh)
        q_lat = jnp.einsum('bthd,rhd->bthr', q, w_uk)
        logits = jnp.einsum('bthr,btkr->bthk', q_lat, c_sel).astype(jnp.float32) * (dh ** -0.5)
        logits = jnp.where(valid[:, :, None, :], logits, -jnp.inf)
        p = jax.nn.softmax(logits, axis=-1).astype(c_sel.dtype)
        o_lat = jnp.einsum('bthk,btkr->bthr', p, c_sel)
        o = jnp.einsum('bthr,rhd->bthd', o_lat, w_uv)
        return o.reshape(B, Q_BLOCK, H * dh)

    cq_blocks = c_q.reshape(B, n_blocks, Q_BLOCK, DSA_Q_RANK).transpose(1, 0, 2, 3)
    w_blocks = w_idx.reshape(B, n_blocks, Q_BLOCK, HI).transpose(1, 0, 2, 3)
    out = lax.map(block, (jnp.arange(n_blocks), cq_blocks, w_blocks))
    out = out.transpose(1, 0, 2, 3).reshape(B, S, H * dh)
    return out @ w_out

def setup_inputs(seed: int = 0) -> dict:
    key = jax.random.key(seed)
    ks = iter(jax.random.split(key, 32))

    def w(shape, fan_in):
        return jax.random.normal(next(ks), shape, jnp.float32) * (fan_in ** -0.5)

    def gain(shape):
        return 1.0 + 0.02 * jax.random.normal(next(ks), shape, jnp.float32)

    NR, ND = N_RET_LAYERS, N_DSA_LAYERS
    return {
        'x': jax.random.normal(next(ks), (BATCH, SEQ, D_MODEL), jnp.float32),
        'norm_ffn1': gain((DEPTH, D_MODEL)),
        'w_ffn1_in': w((DEPTH, D_MODEL, 2 * D_FF), D_MODEL),
        'w_ffn1_out': w((DEPTH, D_FF, D_MODEL), D_FF),
        'norm_mix': gain((DEPTH, D_MODEL)),
        'norm_ffn2': gain((DEPTH, D_MODEL)),
        'w_ffn2_in': w((DEPTH, D_MODEL, 2 * D_FF), D_MODEL),
        'w_ffn2_out': w((DEPTH, D_FF, D_MODEL), D_FF),
        'ret_w_in': w((NR, D_MODEL, RET_IN), D_MODEL),
        'ret_w_out': w((NR, RET_HEADS * RET_DV, D_MODEL), RET_HEADS * RET_DV),
        'dsa_w_in': w((ND, D_MODEL, DSA_IN), D_MODEL),
        'dsa_q_norm': gain((ND, DSA_Q_RANK)),
        'dsa_kv_norm': gain((ND, DSA_KV_RANK)),
        'dsa_w_uq': w((ND, DSA_Q_RANK, DSA_HEADS * DSA_HEAD_DIM), DSA_Q_RANK),
        'dsa_w_qidx': w((ND, DSA_Q_RANK, IDX_HEADS * IDX_DIM), DSA_Q_RANK),
        'dsa_kidx_g': gain((ND, IDX_DIM)),
        'dsa_kidx_b': 0.02 * jax.random.normal(next(ks), (ND, IDX_DIM), jnp.float32),
        'dsa_w_uk': w((ND, DSA_KV_RANK, DSA_HEADS, DSA_HEAD_DIM), DSA_KV_RANK),
        'dsa_w_uv': w((ND, DSA_KV_RANK, DSA_HEADS, DSA_HEAD_DIM), DSA_KV_RANK),
        'dsa_w_out': w((ND, DSA_HEADS * DSA_HEAD_DIM, D_MODEL), DSA_HEADS * DSA_HEAD_DIM),
        'final_norm': gain((D_MODEL,)),
    }

def reference(x, norm_ffn1, w_ffn1_in, w_ffn1_out, norm_mix, norm_ffn2, w_ffn2_in, w_ffn2_out,
              ret_w_in, ret_w_out, dsa_w_in, dsa_q_norm, dsa_kv_norm, dsa_w_uq, dsa_w_qidx,
              dsa_kidx_g, dsa_kidx_b, dsa_w_uk, dsa_w_uv, dsa_w_out, final_norm):
    for layer in range(DEPTH):
        x = x + 0.5 * swiglu(rmsnorm(x, norm_ffn1[layer]), w_ffn1_in[layer], w_ffn1_out[layer])
        h = rmsnorm(x, norm_mix[layer])
        j = layer // N_MIXERS
        if layer % N_MIXERS == 0:
            x = x + retention(h, ret_w_in[j], ret_w_out[j])
        else:
            x = x + dsa_attention(h, dsa_w_in[j], dsa_q_norm[j], dsa_kv_norm[j], dsa_w_uq[j],
                                  dsa_w_qidx[j], dsa_kidx_g[j], dsa_kidx_b[j], dsa_w_uk[j],
                                  dsa_w_uv[j], dsa_w_out[j])
        x = x + 0.5 * swiglu(rmsnorm(x, norm_ffn2[layer]), w_ffn2_in[layer], w_ffn2_out[layer])
    return rmsnorm(x, final_norm)


_drawn_inputs = setup_inputs


def setup_inputs(seed=0):
    import zlib

    import numpy as np

    out = dict(_drawn_inputs(seed))
    spreads = {}
    factors = {'norm_ffn1': 3.043,
     'norm_ffn2': 4.071,
     'dsa_q_norm': 5.059,
     'dsa_kv_norm': 8.0,
     'dsa_kidx_g': 5.427,
     'dsa_kidx_b': 5.04,
     'final_norm': 2.95}
    for name, (base, spread) in spreads.items():
        noise = np.random.default_rng([zlib.crc32(name.encode()), seed]).standard_normal(out[name].shape)
        drawn = base * np.exp(spread * noise) if base else spread * noise
        out[name] = __import__('jax').numpy.asarray(drawn.astype(out[name].dtype))
    for name, factor in factors.items():
        out[name] = (out[name] * factor).astype(out[name].dtype)
    return out
```

```python
from contextlib import ExitStack

import numpy as np

import concourse.bass as bass
from concourse import mybir

P = 128
D_MODEL, SEQ, D_FF = 1024, 512, 2816
EPS = 1e-6
CHUNKS = D_MODEL // P
BLOCKS = SEQ // P
FF_TILES = D_FF // P
RET_HEADS, RET_DK, RET_DV = 4, 256, 512
ROT_BASE = 10000.0
RET_TILES = RET_HEADS * RET_DV // P
V_TILES = RET_DV // P
HEADS, HEAD_DIM = 8, 128
RANK = 256
IDX_HEADS, IDX_DIM = 8, 64
IDX_COLS = IDX_DIM + IDX_HEADS
TOP_K = min(256, SEQ // 4)
MASKED, TAKEN = -3.0e38, -3.4e38
UNSELECTED = -1.0e37

UNIT = 2048
HALF_TILES = FF_TILES // 2
OUT_UNIT = HALF_TILES * P
IDX_UNIT = CHUNKS * IDX_COLS + 2 * 4 * P
FFN_IN_UNITS, FFN_OUT_UNITS = FF_TILES, 2 * CHUNKS
FFN_UNITS = FFN_IN_UNITS + FFN_OUT_UNITS
RET_HEAD_UNITS = 6
RET_IN_UNITS, RET_OUT_UNITS = RET_HEADS * RET_HEAD_UNITS, CHUNKS
DSA_UNITS, DSA_OUT_UNITS = 10, 4
SUBLAYERS = ("ffn", "ret", "ffn", "ffn", "dsa", "ffn")
UNITS_OF = {"ffn": FFN_UNITS, "ret": RET_IN_UNITS + RET_OUT_UNITS, "dsa": DSA_UNITS}
FIRST_UNIT = [sum(UNITS_OF[k] for k in SUBLAYERS[:s]) for s in range(len(SUBLAYERS) + 1)]
TILES_OF = {"ffn": FF_TILES, "ret": RET_TILES, "dsa": 0}
FIRST_TILE = [sum(TILES_OF[k] for k in SUBLAYERS[:s]) for s in range(len(SUBLAYERS) + 1)]
STATS = []
for _s, _kind in enumerate(SUBLAYERS):
    STATS.append(("norm", _s))
    if _kind == "ret":
        STATS += [("head", h) for h in range(RET_HEADS)]
STATS.append(("norm", len(SUBLAYERS)))
SQUARE_OPS = {"norm": 1 + 2 * CHUNKS, "head": V_TILES - 1}

FP32, FP32R = mybir.dt.float32, mybir.dt.float32r
ALU = mybir.AluOpType
ACT = mybir.ActivationFunctionType


def stat_count(which):
    return STATS.index(which) + 1


def broadcast_count(which):
    dsa = ("norm", SUBLAYERS.index("dsa"))
    return len([w for w in STATS[:stat_count(which)] if w != dsa])


def squares_before(which):
    return sum(SQUARE_OPS[kind] for kind, _ in STATS[:STATS.index(which)])


def hybrid_trunk_kernel(nc, x_in, w_ffn_in, w_ffn_out, w_ret_in, w_ret_out, w_dsa, w_dsa_idx,
                        gains_in, rotary_in, decay_in, out):
    with ExitStack() as ctx:
        build(nc, ctx, x_in, w_ffn_in, w_ffn_out, w_ret_in, w_ret_out, w_dsa, w_dsa_idx,
              gains_in, rotary_in, decay_in, out)


def build(nc, ctx, x_in, w_ffn_in, w_ffn_out, w_ret_in, w_ret_out, w_dsa, w_dsa_idx,
          gains_in, rotary_in, decay_in, out):
    top = (nc.sbuf_base + 63) // 64 * 64

    def place(name, width, dtype=FP32):
        nonlocal top
        t = nc.alloc_sbuf_tensor_at(name, [P, width], dtype, offset=top)
        top += (4 * width + 31) // 32 * 32
        return t

    x_res = place("x_res", CHUNKS * SEQ)
    xn_hi = place("xn_hi", CHUNKS * SEQ, FP32R)
    xn_lo = place("xn_lo", CHUNKS * SEQ, FP32R)
    w_raw = [place(f"w_raw{n}", UNIT) for n in range(2)]
    w_hi = [place(f"w_hi{n}", UNIT, FP32R) for n in range(2)]
    w_lo = [place(f"w_lo{n}", UNIT, FP32R) for n in range(2)]
    temp_at = top
    temp = place("temp", 4 * SEQ)
    r_norm = place("r_norm", SEQ)
    square = place("square", SEQ)
    square_sum = place("square_sum", SEQ)
    identity = place("identity", P)
    ones = place("ones", P)
    diagonal = place("diagonal", SEQ)
    GAINS = 7 * CHUNKS + 6
    gains = place("gains", GAINS)
    minus_half = place("minus_half", 16)
    mean_sq = place("mean_sq", BLOCKS)
    r_col = place("r_col", BLOCKS)
    head_r_col = place("head_r_col", BLOCKS)
    arena = top

    gated_hi = place("gated_hi", FF_TILES * SEQ, FP32R)
    gated_lo = place("gated_lo", FF_TILES * SEQ, FP32R)
    rot_cos = place("rot_cos", SEQ)
    rot_sin = place("rot_sin", SEQ)
    decay = place("decay", SEQ)
    after_tables = top

    top = arena
    ret_hi = place("ret_hi", RET_TILES * SEQ, FP32R)
    ret_lo = place("ret_lo", RET_TILES * SEQ, FP32R)
    q_rot = place("q_rot", 2 * SEQ)
    k_rot = place("k_rot", 2 * SEQ)
    v_tok = place("v_tok", BLOCKS * RET_DV)
    from_key = [sum(SEQ - P * i for i in range(j)) for j in range(BLOCKS + 1)]
    to_query = [sum(P * (i + 1) for i in range(b)) for b in range(BLOCKS + 1)]
    scores = place("scores", from_key[BLOCKS])
    r_head = place("r_head", SEQ)
    assert top <= arena + 8 * FF_TILES * SEQ

    top = arena
    q_heads = place("q_heads", HEADS * SEQ)
    o_hi = nc.alloc_sbuf_tensor_at("o_hi", [P, HEADS * SEQ], FP32R, offset=arena)
    k_at = top
    k_heads = place("k_heads", HEADS * SEQ)
    o_lo = nc.alloc_sbuf_tensor_at("o_lo", [P, HEADS * SEQ], FP32R, offset=k_at)
    v_at = top
    v_heads = place("v_heads", BLOCKS * D_MODEL)
    latents = nc.alloc_sbuf_tensor_at("latents", [P, BLOCKS * 2 * RANK], FP32, offset=v_at)
    latent_at = top
    latent_hi = [place(f"latent_hi{n}", SEQ, FP32R) for n in range(4)]
    latent_lo = [place(f"latent_lo{n}", SEQ, FP32R) for n in range(4)]
    k_idx = place("k_idx", SEQ)
    q_idx = place("q_idx", IDX_HEADS * IDX_DIM // P * SEQ)
    idx_scores = place("idx_scores", to_query[BLOCKS])
    select_bias = place("select_bias", to_query[BLOCKS])
    pt_at = top
    probs_t = [place(f"probs_t{n}", from_key[BLOCKS]) for n in range(2)]
    probs = [nc.alloc_sbuf_tensor_at("probs0", [P, to_query[BLOCKS]], FP32, offset=temp_at),
             nc.alloc_sbuf_tensor_at("probs1", [P, to_query[BLOCKS]], FP32, offset=latent_at)]
    k_tok = nc.alloc_sbuf_tensor_at("k_tok", [P, BLOCKS * IDX_DIM], FP32, offset=pt_at)
    k_twice = nc.alloc_sbuf_tensor_at("k_twice", [P, BLOCKS * P], FP32, offset=pt_at + 4 * BLOCKS * IDX_DIM)
    idx_w = place("idx_w", BLOCKS * IDX_HEADS)
    k_mean = place("k_mean", BLOCKS)
    sum_sq = place("sum_sq", 3 * BLOCKS)
    mean_sq3 = place("mean_sq3", 3 * BLOCKS)
    r_col3 = place("r_col3", 3 * BLOCKS)
    best8 = place("best8", 8)
    row_max = place("row_max", 2 * BLOCKS)
    row_sum = place("row_sum", 2 * BLOCKS)

    bank = [ctx.enter_context(nc.psum_tensor(f"bank{n}", [P, SEQ], FP32)) for n in range(8)]

    def sem(name):
        return ctx.enter_context(nc.semaphore(name))

    x_loaded = [sem(f"x_loaded{n}") for n in range(2)]
    tables_loaded = sem("tables_loaded")
    decay_loaded, decay_reloaded = sem("decay_loaded"), sem("decay_reloaded")
    raw_loaded = [sem(f"raw_loaded{n}") for n in range(2)]
    w_hi_made, w_lo_made = sem("w_hi_made"), sem("w_lo_made")
    unit_done = sem("unit_done")
    half_done = sem("half_done")
    x_updated = sem("x_updated")
    xn_hi_made, xn_lo_made = sem("xn_hi_made"), sem("xn_lo_made")
    squares_done = sem("squares_done")
    stat_done = sem("stat_done")
    mean_done = sem("mean_done")
    r_col_done = sem("r_col_done")
    diagonal_done = sem("diagonal_done")
    broadcast_done = sem("broadcast_done")
    r_ready = sem("r_ready")
    temp_filled = sem("temp_filled")
    silu_done = sem("silu_done")
    gated_done = sem("gated_done")
    gated_hi_made, gated_lo_made = sem("gated_hi_made"), sem("gated_lo_made")
    vector_step = sem("vector_step")
    rotary_scaled = sem("rotary_scaled")
    qk_done, qk_rotated = sem("qk_done"), sem("qk_rotated")
    v_scaled = sem("v_scaled")
    scores_done, scores_decayed = sem("scores_done"), sem("scores_decayed")
    ret_out_done = sem("ret_out_done")
    ret_squared = sem("ret_squared")
    consts_made = sem("consts_made")
    latents_copied, latents_squared, latents_scaled = (
        sem("latents_copied"), sem("latents_squared"), sem("latents_scaled"))
    idx_done = sem("idx_done")
    k_copied, k_centred, k_squared, k_scaled = (
        sem("k_copied"), sem("k_centred"), sem("k_squared"), sem("k_scaled"))
    mean3_done, r_col3_done = sem("mean3_done"), sem("r_col3_done")
    latents_turned, k_turned = sem("latents_turned"), sem("k_turned")
    latent_hi_made, latent_lo_made, k_idx_made = (
        sem("latent_hi_made"), sem("latent_lo_made"), sem("k_idx_made"))
    q_idx_done, q_idx_copied = sem("q_idx_done"), sem("q_idx_copied")
    dots_done, relu_done, weighted = sem("dots_done"), sem("relu_done"), sem("weighted")
    causal_done, bias_made = sem("causal_done"), sem("bias_made")
    proj_done, proj_copied = sem("proj_done"), sem("proj_copied")
    logits_done, max_done, exp_done, probs_done = (
        sem("logits_done"), sem("max_done"), sem("exp_done"), sem("probs_done"))
    probs_turned, probs_t_copied = sem("probs_turned"), sem("probs_t_copied")
    o_done, o_hi_made, o_lo_made = sem("o_done"), sem("o_hi_made"), sem("o_lo_made")
    y_done = sem("y_done")
    stored = sem("stored")

    block = ctx.enter_context(nc.Block())

    STAT_BANK = 7
    DSA_BLOCKS = range(TOP_K // P, BLOCKS)
    DOTS = [(b, hh) for b in DSA_BLOCKS for hh in range(IDX_HEADS)]
    DOT_BANKS = (2, 3, 4, 5)
    PROJ_BANKS = (6, 7, 0, 1)
    Q_IDX_TILES = IDX_HEADS * IDX_DIM // P

    def cols(t, i, width=SEQ):
        return t[:, bass.ts(i, width)]

    def tile(t, i):
        return t[:, i * P:(i + 1) * P]

    def unit_size(u):
        for s, kind in enumerate(SUBLAYERS):
            n = u - FIRST_UNIT[s]
            if n < UNITS_OF[kind]:
                if kind == "ffn" and n >= FFN_IN_UNITS:
                    return OUT_UNIT
                return IDX_UNIT if kind == "dsa" and n == 2 else UNIT

    def gain(norm, k):
        return gains[:, bass.ds(norm * CHUNKS + k, 1)]

    def turned_bank(j):
        n, at = ((3, 0), (4, 0), (5, 0), (5, 2 * P))[j]
        return bank[n][:, at:at + SEQ - P * j]

    def logits_bank(b):
        n, at = ((0, 0), (0, P), (1, 0), (2, 0))[b]
        return bank[n][:, at:at + P * (b + 1)]

    @block.sync
    def _(sp):
        def load(u, source, pair=0):
            if u >= 2:
                sp.wait_ge(w_lo_made, u - 1 + 2 * pair)
            sp.dma_start(w_raw[u % 2][:, :source.shape[-1]], source).then_inc(raw_loaded[u % 2], 16)

        for s, kind in enumerate(SUBLAYERS):
            u0 = FIRST_UNIT[s]
            if kind == "ffn":
                f = SUBLAYERS[:s].count("ffn")
                first = 0
                if s == 0:
                    for n in range(2):
                        load(n, w_ffn_in[n])
                    first = 1
                with sp.Fori(0, FFN_IN_UNITS // 2 - first) as i:
                    for n in range(2):
                        load(u0 + 2 * first + n, w_ffn_in[2 * i + (f * FFN_IN_UNITS + 2 * first + n)], i)
                with sp.Fori(0, FFN_OUT_UNITS // 2) as i:
                    for n in range(2):
                        load(u0 + FFN_IN_UNITS + n, w_ffn_out[2 * i + (f * FFN_OUT_UNITS + n)], i)
            elif kind == "ret":
                with sp.Fori(0, RET_IN_UNITS // 2) as i:
                    for n in range(2):
                        load(u0 + n, w_ret_in[2 * i + n], i)
                with sp.Fori(0, RET_OUT_UNITS // 2) as i:
                    for n in range(2):
                        load(u0 + RET_IN_UNITS + n, w_ret_out[2 * i + n], i)
            else:
                for n in range(DSA_UNITS):
                    load(u0 + n, w_dsa_idx if n == 2 else w_dsa[n - (n > 2)])
        for k in range(CHUNKS):
            sp.wait_ge(y_done, k + 1)
            sp.dma_start(out[:, k, :], cols(x_res, k)).then_inc(stored, 16)
        sp.wait_ge(stored, 16 * CHUNKS)

    @block.gpsimd
    def _(pool):
        nc.gpsimd.memset(minus_half[:, :], -0.5).then_inc(consts_made, 1)
        nc.gpsimd.memset(ones[:, :], 1.0).then_inc(consts_made, 1)
        nc.gpsimd.memset(identity[:, :], 0.0).then_inc(consts_made, 1)
        pool.wait_ge(consts_made, 3)
        nc.gpsimd.affine_select(out=identity[:, :], in_=identity[:, :], compare_op=ALU.not_equal,
                                fill=1.0, base=0, pattern=[[-1, P]],
                                channel_multiplier=1).then_inc(consts_made, 1)

        def sum_norm_squares(s, chunk_ready):
            before = squares_before(("norm", s))
            nc.gpsimd.memset(square_sum[:, :], 0.0).then_inc(squares_done, 1)
            def chunk(k):
                chunk_ready(k)
                pool.wait_ge(squares_done, 2 * k + (before + 1))
                nc.gpsimd.tensor_tensor(square[:, :], cols(x_res, k), cols(x_res, k), ALU.mult)\
                    .then_inc(squares_done, 1)
                pool.wait_ge(squares_done, 2 * k + (before + 2))
                nc.gpsimd.tensor_tensor(square_sum[:, :], square_sum[:, :], square[:, :], ALU.add)\
                    .then_inc(squares_done, 1)
            if s == 0:
                for k in range(CHUNKS):
                    chunk(k)
            else:
                with pool.Fori(0, CHUNKS) as k:
                    chunk(k)

        def inverse_rms(which, to):
            pool.wait_ge(mean_done, stat_count(which))
            nc.gpsimd.tensor_tensor(to[:, :], mean_sq[:, :], minus_half[:, :BLOCKS], ALU.pow)\
                .then_inc(r_col_done, 1)

        def half_loaded(k):
            if k in (0, CHUNKS // 2):
                pool.wait_ge(x_loaded[2 * k // CHUNKS], 16)

        sum_norm_squares(0, half_loaded)
        for s, kind in enumerate(SUBLAYERS):
            inverse_rms(("norm", s), r_col)
            if kind == "ret":
                for h in range(RET_HEADS):
                    before = squares_before(("head", h))
                    pool.wait_ge(ret_squared, V_TILES * h + 2)
                    nc.gpsimd.tensor_tensor(square_sum[:, :], cols(temp, 0), cols(temp, 1), ALU.add)\
                        .then_inc(squares_done, 1)
                    for e in range(2, V_TILES):
                        pool.wait_ge(ret_squared, V_TILES * h + e + 1)
                        pool.wait_ge(squares_done, before + e - 1)
                        nc.gpsimd.tensor_tensor(square_sum[:, :], square_sum[:, :], cols(temp, e),
                                                ALU.add).then_inc(squares_done, 1)
                    if h + 1 < RET_HEADS:
                        pool.wait_ge(scores_decayed, BLOCKS * (h + 1))
                        pool.dma_start(decay[:, :], decay_in[h + 1]).then_inc(decay_reloaded, 16)
                    inverse_rms(("head", h), head_r_col)
            if kind == "dsa":
                pool.wait_ge(mean3_done, 2)
                nc.gpsimd.tensor_tensor(r_col3[:, :], mean_sq3[:, :], minus_half[:, :3 * BLOCKS],
                                        ALU.pow).then_inc(r_col3_done, 1)
                nc.gpsimd.memset(select_bias[:, :P], 0.0).then_inc(causal_done, 1)
                pool.wait_ge(causal_done, 1)
                nc.gpsimd.affine_select(out=select_bias[:, :P], in_=select_bias[:, :P],
                                        compare_op=ALU.is_ge, fill=UNSELECTED, base=0,
                                        pattern=[[-1, P]], channel_multiplier=1)\
                    .then_inc(causal_done, 1)
                for n, b in enumerate(DSA_BLOCKS):
                    pool.wait_ge(weighted, IDX_HEADS * (n + 1))
                    own = idx_scores[:, to_query[b + 1] - P:to_query[b + 1]]
                    nc.gpsimd.affine_select(out=own, in_=own, compare_op=ALU.is_ge, fill=MASKED,
                                            base=0, pattern=[[-1, P]], channel_multiplier=1)\
                        .then_inc(causal_done, 1)
            sum_norm_squares(s + 1, lambda k: pool.wait_ge(x_updated, k + (CHUNKS * s + 1)))
        inverse_rms(("norm", len(SUBLAYERS)), r_col)

    @block.scalar
    def _(act):
        copy = ACT.Copy

        def split_unit(u, pair=0):
            size = unit_size(u)
            act.wait_ge(raw_loaded[u % 2], 16 * (u // 2 + 1) + 16 * pair)
            if u >= 2:
                act.wait_ge(unit_done, u - 1 + 2 * pair)
            nc.scalar.activation(w_hi[u % 2][:, :size], w_raw[u % 2][:, :size], copy)\
                .then_inc(w_hi_made, 1)

        def stream_hi(norm, k):
            nc.scalar.activation(cols(xn_hi, k), cols(x_res, k), copy, scale=gain(norm, k))\
                .then_inc(xn_hi_made, 1)

        def copy_broadcast(which, to):
            act.wait_ge(broadcast_done, broadcast_count(which))
            nc.scalar.activation(to[:, :], bank[STAT_BANK][:, :], copy).then_inc(r_ready, 1)

        def gated_tile(count, slot, hi, index):
            gate = cols(temp, 2 * slot)
            act.wait_ge(temp_filled, count)
            nc.scalar.activation(gate, gate, ACT.Silu).then_inc(silu_done, 1)
            act.wait_ge(gated_done, count)
            nc.scalar.activation(cols(hi, index), gate, copy).then_inc(gated_hi_made, 1)

        def residual(s, d):
            act.wait_ge(x_updated, CHUNKS * s + 1 + d)
            stream_hi(s + 1, d)

        act.dma_start(x_res[:, :CHUNKS // 2 * SEQ], x_in[:, :CHUNKS // 2 * SEQ]).then_inc(x_loaded[0], 16)
        act.dma_start(gains[:, :], gains_in).then_inc(tables_loaded, 16)
        act.dma_start(x_res[:, CHUNKS // 2 * SEQ:], x_in[:, CHUNKS // 2 * SEQ:]).then_inc(x_loaded[1], 16)
        act.dma_start(rot_cos[:, :], rotary_in[0]).then_inc(tables_loaded, 16)
        act.dma_start(rot_sin[:, :], rotary_in[1]).then_inc(tables_loaded, 16)
        act.dma_start(decay[:, :], decay_in[0]).then_inc(decay_loaded, 16)
        act.wait_ge(tables_loaded, 48)
        for k in range(CHUNKS):
            if k in (0, CHUNKS // 2):
                act.wait_ge(x_loaded[2 * k // CHUNKS], 16)
            stream_hi(0, k)
            if k in (0, CHUNKS // 2):
                split_unit(2 * k // CHUNKS)

        for s, kind in enumerate(SUBLAYERS):
            u0, tile0 = FIRST_UNIT[s], FIRST_TILE[s]
            last = s == len(SUBLAYERS) - 1
            if kind == "ffn":
                def in_pair(first, pair):
                    for n in range(2):
                        step = 2 * first + n
                        split_unit(u0 + step + 2, pair)
                        if step == 0:
                            copy_broadcast(("norm", s), r_norm)
                        gated_tile(tile0 + step + 1 + 2 * pair, n, gated_hi, step + 2 * pair)

                in_pair(0, 0)
                with act.Fori(0, FFN_IN_UNITS // 2 - 2) as i:
                    in_pair(1, i)
                in_pair(FFN_IN_UNITS // 2 - 1, 0)

                def out_tile(first, i):
                    for n in range(2):
                        if last and first == CHUNKS - 1:
                            continue
                        split_unit(u0 + FFN_IN_UNITS + 2 * first + n + 2, i)
                    if not last:
                        residual(s, first + i)

                with act.Fori(0, CHUNKS - 1) as i:
                    out_tile(0, i)
                out_tile(CHUNKS - 1, 0)
            elif kind == "ret":
                for h in range(RET_HEADS):
                    u = u0 + RET_HEAD_UNITS * h
                    if h == 0:
                        split_unit(u + 2)
                        copy_broadcast(("norm", s), r_norm)
                    else:
                        split_unit(u + 2)
                    split_unit(u + 3)
                    split_unit(u + 4)
                    act.wait_ge(unit_done, u + 4)
                    for b in range(BLOCKS):
                        nc.scalar.activation(cols(v_tok, b), bank[b][:, :], copy,
                                             scale=r_col[:, b:b + 1]).then_inc(v_scaled, 1)
                    split_unit(u + 5)
                    for e in range(V_TILES):
                        act.wait_ge(ret_out_done, V_TILES * h + e + 1)
                        nc.scalar.activation(cols(temp, e), bank[e][:, :], ACT.Square)\
                            .then_inc(ret_squared, 1)
                    copy_broadcast(("head", h), r_head)
                    for e in range(V_TILES):
                        if e % 2 == 1:
                            split_unit(u + 6 + e // 2)
                        n = V_TILES * h + e
                        gated_tile(tile0 + n + 1, e % 2, ret_hi, n)
                with act.Fori(0, CHUNKS // 2 - 1) as i:
                    for n in range(2):
                        split_unit(u0 + RET_IN_UNITS + 2 + n, i)
                        residual(s, 2 * i + n)
                for n in range(2):
                    split_unit(FIRST_UNIT[s + 1] + n)
                    residual(s, CHUNKS - 2 + n)
            else:
                split_unit(u0 + 2)
                act.wait_ge(r_col_done, stat_count(("norm", s)))
                act.wait_ge(unit_done, u0 + 2)
                for b in range(BLOCKS):
                    nc.scalar.activation(cols(latents, b), bank[b][:, :], copy,
                                         scale=r_col[:, b:b + 1]).then_inc(latents_copied, 1)
                split_unit(u0 + 3)
                act.wait_ge(idx_done, 1)
                for b in range(BLOCKS):
                    nc.scalar.activation(cols(k_tok, b, IDX_DIM),
                                         bank[4][:, b * IDX_COLS:b * IDX_COLS + IDX_DIM], copy,
                                         scale=r_col[:, b:b + 1], accum_out=k_mean[:, b:b + 1])\
                        .then_inc(k_copied, 1)
                act.wait_ge(latents_copied, BLOCKS)
                for b in range(BLOCKS):
                    for n in range(2):
                        nc.scalar.activation(cols(temp, 2 * b + n, RANK), cols(latents, 2 * b + n, RANK),
                                             ACT.Square, accum_out=sum_sq[:, 2 * b + n:2 * b + n + 1])\
                            .then_inc(latents_squared, 1)
                act.wait_ge(k_centred, BLOCKS)
                for b in range(BLOCKS):
                    nc.scalar.activation(cols(diagonal, b, IDX_DIM), cols(k_tok, b, IDX_DIM), ACT.Square,
                                         accum_out=sum_sq[:, 2 * BLOCKS + b:2 * BLOCKS + b + 1])\
                        .then_inc(k_squared, 1)
                for n in range(4):
                    act.wait_ge(latents_turned, n + 1)
                    nc.scalar.activation(latent_hi[n][:, :], bank[n][:, :], copy,
                                         scale=gains[:, 7 * CHUNKS + n:7 * CHUNKS + n + 1])\
                        .then_inc(latent_hi_made, 1)
                for m in range(Q_IDX_TILES):
                    if m < Q_IDX_TILES - 1:
                        act.wait_ge(q_idx_done, m + 1)
                    else:
                        act.wait_ge(unit_done, u0 + 3)
                    nc.scalar.activation(cols(q_idx, m), bank[PROJ_BANKS[m]][:, :], copy)\
                        .then_inc(q_idx_copied, 1)
                split_unit(u0 + 4)
                for c, (b, hh) in enumerate(DOTS):
                    keys = P * (b + 1)
                    act.wait_ge(dots_done, c + 1)
                    if c >= 4:
                        act.wait_ge(weighted, c - 3)
                    nc.scalar.activation(cols(temp, c % 4)[:, :keys], bank[DOT_BANKS[c % 4]][:, :keys],
                                         ACT.Relu, scale=IDX_DIM ** -0.5).then_inc(relu_done, 1)
                for j in range(3 * 8):
                    if j % 8 < 7:
                        act.wait_ge(proj_done, 7 * (j // 8) + j % 8 + 1)
                    else:
                        act.wait_ge(unit_done, u0 + 4 + j // 8)
                    to = (q_heads, k_heads, v_heads)[j // 8]
                    nc.scalar.activation(cols(to, j % 8), bank[PROJ_BANKS[j % 4]][:, :], copy)\
                        .then_inc(proj_copied, 1)
                    if j % 8 == 7:
                        split_unit(u0 + 5 + j // 8)

                def exps(h):
                    for b in range(BLOCKS):
                        n = BLOCKS * (h % 2) + b
                        if b == 0:
                            act.wait_ge(max_done, h + 1)
                        part = probs[h % 2][:, to_query[b]:to_query[b + 1]]
                        nc.scalar.activation(part, part, ACT.Exp, bias=row_max[:, n:n + 1],
                                             accum_out=row_sum[:, n:n + 1]).then_inc(exp_done, 1)

                def copy_probs_t(h):
                    act.wait_ge(probs_turned, h + 1)
                    if h >= 2:
                        act.wait_ge(o_done, h - 1)
                    for j in range(BLOCKS):
                        nc.scalar.activation(probs_t[h % 2][:, from_key[j]:from_key[j + 1]],
                                             turned_bank(j), copy).then_inc(probs_t_copied, 1)

                def result_hi(h):
                    act.wait_ge(o_done, h + 1)
                    nc.scalar.activation(cols(o_hi, h), bank[6 + h % 2][:, :], copy)\
                        .then_inc(o_hi_made, 1)

                exps(0)
                for h in range(HEADS):
                    if h + 1 < HEADS:
                        exps(h + 1)
                    copy_probs_t(h)
                    if h >= 1:
                        result_hi(h - 1)
                result_hi(HEADS - 1)
                for d in range(CHUNKS):
                    if d % 2 == 1:
                        split_unit(u0 + DSA_UNITS - DSA_OUT_UNITS + 2 + d // 2)
                    residual(s, d)
        copy_broadcast(("norm", len(SUBLAYERS)), r_norm)

    @block.vector
    def _(dve):
        steps = [0]

        def link(instruction):
            steps[0] += 1
            instruction.then_inc(vector_step, 1)
            dve.wait_ge(vector_step, steps[0])

        def split_unit(u, pair=0):
            size = unit_size(u)
            dve.wait_ge(w_hi_made, u + 1 + 2 * pair)
            nc.vector.tensor_tensor(w_lo[u % 2][:, :size], w_raw[u % 2][:, :size],
                                    w_hi[u % 2][:, :size].bitcast(FP32), ALU.subtract)\
                .then_inc(w_lo_made, 1)

        def stream_lo(norm, k):
            dve.wait_ge(xn_hi_made, CHUNKS * norm + 1 + k)
            nc.vector.scalar_tensor_tensor(cols(xn_lo, k), cols(x_res, k), gain(norm, k),
                                           cols(xn_hi, k).bitcast(FP32), ALU.mult, ALU.subtract)\
                .then_inc(xn_lo_made, 1)

        def mean_square(which, width):
            dve.wait_ge(stat_done, stat_count(which))
            nc.vector.tensor_scalar(mean_sq[:, :], bank[STAT_BANK][:, :BLOCKS], 1.0 / width, EPS,
                                    ALU.mult, ALU.add).then_inc(mean_done, 1)

        def spread(which, r):
            dve.wait_ge(r_col_done, stat_count(which))
            for b in range(BLOCKS):
                last = nc.vector.tensor_scalar(tile(diagonal, b), identity[:, :], r[:, b:b + 1], None,
                                               ALU.mult)
            last.then_inc(diagonal_done, 1)

        def fill_temp(slot, gate, value, factor):
            nc.vector.tensor_tensor(cols(temp, 2 * slot), gate[:, :], r_norm[:, :], ALU.mult)
            nc.vector.tensor_tensor(cols(temp, 2 * slot + 1), value[:, :], factor[:, :], ALU.mult)\
                .then_inc(temp_filled, 1)

        def gated_tile(count, slot, hi, lo, index):
            gate = cols(temp, 2 * slot)
            dve.wait_ge(silu_done, count)
            nc.vector.tensor_tensor(gate, gate, cols(temp, 2 * slot + 1), ALU.mult)\
                .then_inc(gated_done, 1)
            dve.wait_ge(gated_hi_made, count)
            nc.vector.tensor_tensor(cols(lo, index), gate, cols(hi, index).bitcast(FP32),
                                    ALU.subtract).then_inc(gated_lo_made, 1)

        def update(s, d, n, factor):
            nc.vector.scalar_tensor_tensor(cols(x_res, d), bank[4 + n][:, :], factor, cols(x_res, d),
                                           ALU.mult, ALU.add).then_inc(x_updated, 1)

        dve.wait_ge(tables_loaded, 48)
        dve.wait_ge(consts_made, 4)
        for k in range(CHUNKS):
            stream_lo(0, k)
            if k in (0, CHUNKS // 2):
                split_unit(2 * k // CHUNKS)

        for s, kind in enumerate(SUBLAYERS):
            u0, tile0 = FIRST_UNIT[s], FIRST_TILE[s]
            last = s == len(SUBLAYERS) - 1
            if kind != "dsa":
                mean_square(("norm", s), D_MODEL)
                spread(("norm", s), r_col)
            if kind == "ffn":
                def in_pair(first, pair):
                    for n in range(2):
                        step = 2 * first + n
                        if step == 0:
                            dve.wait_ge(r_ready, broadcast_count(("norm", s)))
                        dve.wait_ge(unit_done, u0 + step + 1 + 2 * pair)
                        fill_temp(n, bank[2 * n], bank[2 * n + 1], r_norm)
                        split_unit(u0 + step + 2, pair)
                        gated_tile(tile0 + step + 1 + 2 * pair, n, gated_hi, gated_lo, step + 2 * pair)

                in_pair(0, 0)
                with dve.Fori(0, FFN_IN_UNITS // 2 - 2) as i:
                    in_pair(1, i)
                in_pair(FFN_IN_UNITS // 2 - 1, 0)

                def out_tile(d, n, pair):
                    u = u0 + FFN_IN_UNITS + 2 * d
                    at_end = last and d == CHUNKS - 1
                    if not at_end:
                        split_unit(u + 2, pair)
                    dve.wait_ge(unit_done, u + 2 + 2 * pair)
                    update(s, d + pair, n, 0.5)
                    if not at_end:
                        split_unit(u + 3, pair)
                    if not last:
                        stream_lo(s + 1, d + pair)

                with dve.Fori(0, CHUNKS // 2 - 1) as i:
                    for n in range(2):
                        out_tile(n, n, 2 * i)
                for n in range(2):
                    out_tile(CHUNKS - 2 + n, n, 0)
            elif kind == "ret":
                dve.wait_ge(r_ready, broadcast_count(("norm", s)))
                nc.vector.tensor_tensor(rot_cos[:, :], rot_cos[:, :], r_norm[:, :], ALU.mult)
                link(nc.vector.tensor_tensor(rot_sin[:, :], rot_sin[:, :], r_norm[:, :], ALU.mult))

                def rotate(to, even, odd):
                    for n, (a, b, op) in enumerate(((even, odd, ALU.subtract), (odd, even, ALU.add))):
                        nc.vector.tensor_tensor(cols(temp, 2 * n), a[:, :], rot_cos[:, :], ALU.mult)
                        link(nc.vector.tensor_tensor(cols(temp, 2 * n + 1), b[:, :], rot_sin[:, :],
                                                     ALU.mult))
                        done = nc.vector.tensor_tensor(cols(to, n), cols(temp, 2 * n),
                                                       cols(temp, 2 * n + 1), op)
                    done.then_inc(qk_rotated, 1)

                for h in range(RET_HEADS):
                    u = u0 + RET_HEAD_UNITS * h
                    for n, to in enumerate((q_rot, k_rot)):
                        split_unit(u + 2 + n)
                        dve.wait_ge(unit_done, u + 1 + n)
                        rotate(to, bank[4 + 2 * n], bank[5 + 2 * n])
                    split_unit(u + 4)
                    split_unit(u + 5)
                    if h == 0:
                        dve.wait_ge(decay_loaded, 16)
                    else:
                        dve.wait_ge(decay_reloaded, 16 * h)
                    for j in range(BLOCKS):
                        width = SEQ - P * j
                        dve.wait_ge(scores_done, BLOCKS * h + j + 1)
                        nc.vector.tensor_tensor(scores[:, from_key[j]:from_key[j + 1]],
                                                bank[4 + j][:, :width], decay[:, :width], ALU.mult)\
                            .then_inc(scores_decayed, 1)
                    mean_square(("head", h), RET_DV)
                    spread(("head", h), head_r_col)
                    dve.wait_ge(r_ready, broadcast_count(("head", h)))
                    for e in range(V_TILES):
                        n = V_TILES * h + e
                        if e % 2 == 0:
                            dve.wait_ge(half_done, n // 2 + 1)
                        else:
                            dve.wait_ge(unit_done, u + 5 + e // 2)
                        fill_temp(e % 2, bank[4 + e % 3], bank[e], r_head)
                        if e % 2 == 1:
                            split_unit(u + 6 + e // 2)
                        gated_tile(tile0 + n + 1, e % 2, ret_hi, ret_lo, n)

                def out_tile(d, n, pair):
                    u = u0 + RET_IN_UNITS + d
                    dve.wait_ge(unit_done, u + 1 + 2 * pair)
                    update(s, d + 2 * pair, n, 1.0)
                    split_unit(u + 2, pair)
                    stream_lo(s + 1, d + 2 * pair)

                with dve.Fori(0, CHUNKS // 2 - 1) as i:
                    for n in range(2):
                        out_tile(n, n, i)
                for n in range(2):
                    out_tile(CHUNKS - 2 + n, n, 0)
            else:
                mean_square(("norm", s), D_MODEL)
                split_unit(u0 + 2)
                split_unit(u0 + 3)
                dve.wait_ge(r_col_done, stat_count(("norm", s)))
                dve.wait_ge(k_copied, BLOCKS)
                for b in range(BLOCKS):
                    nc.vector.tensor_scalar(cols(idx_w, b, IDX_HEADS),
                                            bank[4][:, b * IDX_COLS + IDX_DIM:(b + 1) * IDX_COLS],
                                            r_col[:, b:b + 1], IDX_HEADS ** -0.5, ALU.mult, ALU.mult)
                link(nc.vector.tensor_scalar(k_mean[:, :], k_mean[:, :], 1.0 / IDX_DIM, None, ALU.mult))
                for b in range(BLOCKS):
                    nc.vector.tensor_scalar(cols(k_tok, b, IDX_DIM), cols(k_tok, b, IDX_DIM),
                                            k_mean[:, b:b + 1], None, ALU.subtract)\
                        .then_inc(k_centred, 1)
                dve.wait_ge(latents_squared, 2 * BLOCKS)
                nc.vector.tensor_scalar(mean_sq3[:, :2 * BLOCKS], sum_sq[:, :2 * BLOCKS], 1.0 / RANK, EPS,
                                        ALU.mult, ALU.add).then_inc(mean3_done, 1)
                dve.wait_ge(k_squared, BLOCKS)
                nc.vector.tensor_scalar(mean_sq3[:, 2 * BLOCKS:], sum_sq[:, 2 * BLOCKS:], 1.0 / IDX_DIM,
                                        EPS, ALU.mult, ALU.add).then_inc(mean3_done, 1)
                dve.wait_ge(r_col3_done, 1)
                for b in range(BLOCKS):
                    for n in range(2):
                        part = cols(latents, 2 * b + n, RANK)
                        nc.vector.tensor_scalar(part, part, r_col3[:, 2 * b + n:2 * b + n + 1], None,
                                                ALU.mult).then_inc(latents_scaled, 1)
                for b in range(BLOCKS):
                    for n in range(2):
                        nc.vector.tensor_scalar(cols(k_twice, 2 * b + n, IDX_DIM), cols(k_tok, b, IDX_DIM),
                                                r_col3[:, 2 * BLOCKS + b:2 * BLOCKS + b + 1], None,
                                                ALU.mult).then_inc(k_scaled, 1)
                for n in range(4):
                    dve.wait_ge(latent_hi_made, n + 1)
                    nc.vector.scalar_tensor_tensor(latent_lo[n][:, :], bank[n][:, :],
                                                   gains[:, 7 * CHUNKS + n:7 * CHUNKS + n + 1],
                                                   latent_hi[n][:, :].bitcast(FP32), ALU.mult,
                                                   ALU.subtract).then_inc(latent_lo_made, 1)
                dve.wait_ge(k_turned, 1)
                nc.vector.tensor_scalar(k_idx[:, :], bank[5][:, :], gains[:, 7 * CHUNKS + 4:7 * CHUNKS + 5],
                                        gains[:, 7 * CHUNKS + 5:7 * CHUNKS + 6], ALU.mult, ALU.add)\
                    .then_inc(k_idx_made, 1)
                split_unit(u0 + 4)
                for c, (b, hh) in enumerate(DOTS):
                    keys = P * (b + 1)
                    to = idx_scores[:, to_query[b]:to_query[b + 1]]
                    head_w = idx_w[:, b * IDX_HEADS + hh:b * IDX_HEADS + hh + 1]
                    dve.wait_ge(relu_done, c + 1)
                    if hh == 0:
                        nc.vector.tensor_scalar(to, cols(temp, c % 4)[:, :keys], head_w, None, ALU.mult)\
                            .then_inc(weighted, 1)
                    else:
                        dve.wait_ge(weighted, c)
                        nc.vector.scalar_tensor_tensor(to, cols(temp, c % 4)[:, :keys], head_w, to,
                                                       ALU.mult, ALU.add).then_inc(weighted, 1)
                for n, b in enumerate(DSA_BLOCKS):
                    part = idx_scores[:, to_query[b]:to_query[b + 1]]
                    dve.wait_ge(causal_done, n + 3)
                    for _ in range(TOP_K // 8):
                        link(nc.vector.max(best8[:, :], part))
                        link(nc.vector.match_replace(part, best8[:, :], part, TAKEN))
                    nc.vector.tensor_scalar(select_bias[:, to_query[b]:to_query[b + 1]], part,
                                            (MASKED + TAKEN) / 2, UNSELECTED, ALU.is_gt, ALU.mult)\
                        .then_inc(bias_made, 1)
                    split_unit(u0 + 5 + n)

                def maxima(h):
                    dve.wait_ge(logits_done, h + 1)
                    if h >= 2:
                        dve.wait_ge(probs_turned, h - 1)
                    for b in range(BLOCKS):
                        n = BLOCKS * (h % 2) + b
                        done = nc.vector.tensor_tensor_reduce(
                            out=probs[h % 2][:, to_query[b]:to_query[b + 1]], in0=logits_bank(b),
                            in1=select_bias[:, to_query[b]:to_query[b + 1]], scale=HEAD_DIM ** -0.5,
                            scalar=UNSELECTED, op0=ALU.add, op1=ALU.max, accum_out=row_max[:, n:n + 1])
                    link(done)
                    n = BLOCKS * (h % 2)
                    nc.vector.tensor_scalar(row_max[:, n:n + BLOCKS], row_max[:, n:n + BLOCKS], -1.0,
                                            None, ALU.mult).then_inc(max_done, 1)

                def normalise(h):
                    dve.wait_ge(exp_done, BLOCKS * (h + 1))
                    n = BLOCKS * (h % 2)
                    link(nc.vector.reciprocal(row_sum[:, n:n + BLOCKS], row_sum[:, n:n + BLOCKS]))
                    for b in range(BLOCKS):
                        part = probs[h % 2][:, to_query[b]:to_query[b + 1]]
                        nc.vector.tensor_scalar(part, part, row_sum[:, n + b:n + b + 1], None,
                                                ALU.mult).then_inc(probs_done, 1)

                def result_lo(h):
                    dve.wait_ge(o_hi_made, h + 1)
                    nc.vector.tensor_tensor(cols(o_lo, h), bank[6 + h % 2][:, :],
                                            cols(o_hi, h).bitcast(FP32), ALU.subtract)\
                        .then_inc(o_lo_made, 1)

                dve.wait_ge(bias_made, len(DSA_BLOCKS))
                maxima(0)
                for h in range(HEADS):
                    if h + 1 < HEADS:
                        maxima(h + 1)
                    normalise(h)
                    if h >= 1:
                        result_lo(h - 1)
                result_lo(HEADS - 1)
                for d in range(CHUNKS):
                    u = u0 + DSA_UNITS - DSA_OUT_UNITS + d // 2
                    if d % 2 == 0:
                        dve.wait_ge(half_done, 2 * RET_HEADS + d // 2 + 1)
                    else:
                        dve.wait_ge(unit_done, u + 1)
                    update(s, d, d % 2, 1.0)
                    if d % 2 == 1:
                        split_unit(u + 2)
                    stream_lo(s + 1, d)
        final = len(SUBLAYERS)
        mean_square(("norm", final), D_MODEL)
        spread(("norm", final), r_col)
        dve.wait_ge(r_ready, broadcast_count(("norm", final)))
        for k in range(CHUNKS):
            nc.vector.scalar_tensor_tensor(cols(x_res, k), cols(x_res, k), gain(final, k), r_norm[:, :],
                                           ALU.mult, ALU.mult).then_inc(y_done, 1)

    @block.tensor
    def _(pe):
        mm = nc.tensor.matmul

        def product(to, slot, at, hi, lo, start, stop):
            mm(to, w_hi[slot][:, at:at + P], hi, start=start, stop=False)
            mm(to, w_hi[slot][:, at:at + P], lo, start=False, stop=False)
            return mm(to, w_lo[slot][:, at:at + P], hi, start=False, stop=stop)

        def product_by_token(to, hi, lo, slot, at, width, start, stop):
            mm(to, hi, w_hi[slot][:, at:at + width], start=start, stop=False)
            mm(to, hi, w_lo[slot][:, at:at + width], start=False, stop=False)
            return mm(to, lo, w_hi[slot][:, at:at + width], start=False, stop=stop)

        def from_stream(to, slot, first_tile, ready=None):
            for k in range(CHUNKS):
                if ready is not None:
                    pe.wait_ge(xn_lo_made, ready + k + 1)
                done = product(to[:, :], slot, (first_tile + k) * P, cols(xn_hi, k), cols(xn_lo, k),
                               k == 0, k == CHUNKS - 1)
            return done

        def sum_over_features(which):
            pe.wait_ge(squares_done, squares_before(which) + SQUARE_OPS[which[0]])
            for b in range(BLOCKS):
                done = mm(bank[STAT_BANK][:, b:b + 1], tile(square_sum, b), ones[:, :1], start=True,
                          stop=True)
            done.then_inc(stat_done, 1)

        def broadcast(which):
            pe.wait_ge(diagonal_done, broadcast_count(which))
            mm(bank[STAT_BANK][:, :], ones[:, :], diagonal[:, :], start=True, stop=True)\
                .then_inc(broadcast_done, 1)

        pe.wait_ge(consts_made, 4)
        for s, kind in enumerate(SUBLAYERS):
            u0, tile0 = FIRST_UNIT[s], FIRST_TILE[s]
            norm = ("norm", s)
            if kind == "ffn":
                def in_pair(first, pair):
                    for n in range(2):
                        step = 2 * first + n
                        pe.wait_ge(w_lo_made, u0 + step + 1 + 2 * pair)
                        if step >= 2:
                            pe.wait_ge(temp_filled, tile0 + step - 1 + 2 * pair)
                        from_stream(bank[2 * n], n, 0, CHUNKS * s if step == 0 else None)
                        if step == 0:
                            sum_over_features(norm)
                        from_stream(bank[2 * n + 1], n, CHUNKS).then_inc(unit_done, 1)
                        if step == 0:
                            broadcast(norm)

                in_pair(0, 0)
                with pe.Fori(0, FFN_IN_UNITS // 2 - 1) as i:
                    in_pair(1, i)

                def out_tile(d, n, pair):
                    if d >= 2:
                        pe.wait_ge(x_updated, CHUNKS * s + d - 1 + pair)
                    for half in range(2):
                        pe.wait_ge(w_lo_made, u0 + FFN_IN_UNITS + 2 * d + half + 1 + 2 * pair)
                        for kk in range(HALF_TILES):
                            k = HALF_TILES * half + kk
                            if d == 0:
                                pe.wait_ge(gated_lo_made, tile0 + k + 1)
                            done = product(bank[4 + n][:, :], half, kk * P, cols(gated_hi, k),
                                           cols(gated_lo, k), k == 0, k == FF_TILES - 1)
                        done.then_inc(unit_done, 1)

                for n in range(2):
                    out_tile(n, n, 0)
                with pe.Fori(0, CHUNKS // 2 - 1) as i:
                    for n in range(2):
                        out_tile(2 + n, n, 2 * i)
            elif kind == "ret":
                for h in range(RET_HEADS):
                    u = u0 + RET_HEAD_UNITS * h
                    for n in range(2):
                        pe.wait_ge(w_lo_made, u + 1 + n)
                        if n == 0 and h > 0:
                            pe.wait_ge(temp_filled, tile0 + V_TILES * h)
                        from_stream(bank[4 + 2 * n], n, 0, CHUNKS * s if h == 0 and n == 0 else None)
                        if h == 0 and n == 0:
                            sum_over_features(norm)
                        if h == 0 and n == 1:
                            pe.wait_ge(r_ready, broadcast_count(norm))
                        from_stream(bank[5 + 2 * n], n, CHUNKS).then_inc(unit_done, 1)
                        if h == 0 and n == 0:
                            broadcast(norm)
                    for half in range(2):
                        pe.wait_ge(w_lo_made, u + 3 + half)
                        for kk in range(CHUNKS // 2):
                            k = CHUNKS // 2 * half + kk
                            for b in range(BLOCKS):
                                done = product_by_token(
                                    bank[b][:, :], tile(xn_hi, k * BLOCKS + b),
                                    tile(xn_lo, k * BLOCKS + b), half, kk * RET_DV, RET_DV,
                                    k == 0, k == CHUNKS - 1)
                        done.then_inc(unit_done, 1)
                    pe.wait_ge(qk_rotated, 2 * h + 2)
                    for j in range(BLOCKS):
                        for n in range(2):
                            done = mm(bank[4 + j][:, :SEQ - P * j], tile(k_rot, n * BLOCKS + j),
                                      q_rot[:, n * SEQ + P * j:(n + 1) * SEQ], start=n == 0,
                                      stop=n == 1)
                        done.then_inc(scores_done, 1)
                    pe.wait_ge(v_scaled, BLOCKS * (h + 1))
                    for e in range(V_TILES):
                        for j in range(BLOCKS):
                            if e == 0:
                                pe.wait_ge(scores_decayed, BLOCKS * h + j + 1)
                            done = mm(bank[e][:, P * j:], tile(v_tok, j * V_TILES + e),
                                      scores[:, from_key[j]:from_key[j + 1]], start=j == 0,
                                      stop=j == BLOCKS - 1)
                        done.then_inc(ret_out_done, 1)
                    for e in range(V_TILES):
                        if e % 2 == 0:
                            pe.wait_ge(w_lo_made, u + 5 + e // 2)
                        if e == 3:
                            pe.wait_ge(temp_filled, tile0 + V_TILES * h + 1)
                        from_stream(bank[4 + e % 3], e // 2, e % 2 * CHUNKS)\
                            .then_inc(unit_done if e % 2 else half_done, 1)
                        if e == 0:
                            sum_over_features(("head", h))
                        if e == 1:
                            broadcast(("head", h))

                def out_tile(d, n, pair):
                    if d >= 2:
                        pe.wait_ge(x_updated, CHUNKS * s + d - 1 + pair)
                    pe.wait_ge(w_lo_made, u0 + RET_IN_UNITS + d + 1 + pair)
                    for k in range(RET_TILES):
                        if d == 0:
                            pe.wait_ge(gated_lo_made, tile0 + k + 1)
                        done = product(bank[4 + n][:, :], n, k * P, cols(ret_hi, k), cols(ret_lo, k),
                                       k == 0, k == RET_TILES - 1)
                    done.then_inc(unit_done, 1)

                pe.wait_ge(temp_filled, tile0 + RET_TILES)
                for n in range(2):
                    out_tile(n, n, 0)
                with pe.Fori(0, CHUNKS // 2 - 1) as i:
                    for n in range(2):
                        out_tile(2 + n, n, 2 * i)
            else:
                for half in range(2):
                    pe.wait_ge(w_lo_made, u0 + 1 + half)
                    for kk in range(CHUNKS // 2):
                        k = CHUNKS // 2 * half + kk
                        pe.wait_ge(xn_lo_made, CHUNKS * s + k + 1)
                        for b in range(BLOCKS):
                            done = product_by_token(
                                bank[b][:, :], tile(xn_hi, k * BLOCKS + b), tile(xn_lo, k * BLOCKS + b),
                                half, kk * 2 * RANK, 2 * RANK, k == 0, k == CHUNKS - 1)
                    done.then_inc(unit_done, 1)
                    if half == 0:
                        sum_over_features(norm)
                pe.wait_ge(w_lo_made, u0 + 3)
                for b in range(BLOCKS):
                    for k in range(CHUNKS):
                        done = product_by_token(
                            bank[4][:, b * IDX_COLS:(b + 1) * IDX_COLS], tile(xn_hi, k * BLOCKS + b),
                            tile(xn_lo, k * BLOCKS + b), 0, k * IDX_COLS, IDX_COLS, k == 0,
                            k == CHUNKS - 1)
                done.then_inc(idx_done, 1)
                pe.wait_ge(latents_scaled, 2 * BLOCKS)
                for n in range(4):
                    for b in range(BLOCKS):
                        done = nc.tensor.transpose(tile(bank[n], b), tile(latents, b * 4 + n),
                                                   identity[:, :])
                    done.then_inc(latents_turned, 1)
                pe.wait_ge(k_scaled, 2 * BLOCKS)
                for b in range(BLOCKS):
                    done = nc.tensor.transpose(tile(bank[5], b), tile(k_twice, b), identity[:, :])
                done.then_inc(k_turned, 1)
                pe.wait_ge(latent_lo_made, 2)
                for m in range(Q_IDX_TILES):
                    for n in range(2):
                        done = product(bank[PROJ_BANKS[m]][:, :], 0,
                                       CHUNKS * IDX_COLS + (n * Q_IDX_TILES + m) * P,
                                       latent_hi[n][:, :], latent_lo[n][:, :], n == 0, n == 1)
                    done.then_inc(q_idx_done if m < Q_IDX_TILES - 1 else unit_done, 1)
                pe.wait_ge(k_idx_made, 1)
                pe.wait_ge(latent_lo_made, 4)
                pe.wait_ge(q_idx_copied, Q_IDX_TILES)
                for c, (b, hh) in enumerate(DOTS):
                    keys, at = P * (b + 1), IDX_DIM * (hh % 2)
                    if c >= 4:
                        pe.wait_ge(relu_done, c - 3)
                    mm(bank[DOT_BANKS[c % 4]][:, :keys],
                       q_idx[at:at + IDX_DIM, hh // 2 * SEQ + b * P:hh // 2 * SEQ + (b + 1) * P],
                       k_idx[at:at + IDX_DIM, :keys], start=True, stop=True).then_inc(dots_done, 1)
                for j in range(3 * 8):
                    slot = (u0 + 3 + j // 8) % 2
                    if j % 8 == 0:
                        pe.wait_ge(w_lo_made, u0 + 4 + j // 8)
                    if j >= 4:
                        pe.wait_ge(proj_copied, j - 3)
                    to = bank[PROJ_BANKS[j % 4]][:, :]
                    for n in range(2):
                        if j < 16:
                            lat = 2 * (j // 8) + n
                            done = product(to, slot, (j % 8 * 2 + n) * P, latent_hi[lat][:, :],
                                           latent_lo[lat][:, :], n == 0, n == 1)
                        else:
                            b, half = (j - 16) // 2, j % 2
                            done = product_by_token(to, tile(latent_hi[2 + n], b),
                                                    tile(latent_lo[2 + n], b), slot,
                                                    n * D_MODEL + half * SEQ, SEQ, n == 0, n == 1)
                    done.then_inc(unit_done if j % 8 == 7 else proj_done, 1)

                def logits(h):
                    if h >= 1:
                        pe.wait_ge(max_done, h)
                    for b in range(BLOCKS):
                        done = mm(logits_bank(b), tile(q_heads, h * BLOCKS + b),
                                  k_heads[:, h * SEQ:h * SEQ + P * (b + 1)], start=True, stop=True)
                    done.then_inc(logits_done, 1)

                def turn_probs(h):
                    pe.wait_ge(probs_done, BLOCKS * (h + 1))
                    if h >= 1:
                        pe.wait_ge(probs_t_copied, BLOCKS * h)
                    for j in range(BLOCKS):
                        for b in range(j, BLOCKS):
                            at = to_query[b] + j * P
                            done = nc.tensor.transpose(tile(turned_bank(j), b - j),
                                                       probs[h % 2][:, at:at + P], identity[:, :])
                    done.then_inc(probs_turned, 1)

                def results(h):
                    pe.wait_ge(probs_t_copied, BLOCKS * (h + 1))
                    if h >= 2:
                        pe.wait_ge(o_lo_made, h - 1)
                    for j in range(BLOCKS):
                        done = mm(bank[6 + h % 2][:, P * j:], tile(v_heads, j * HEADS + h),
                                  probs_t[h % 2][:, from_key[j]:from_key[j + 1]], start=j == 0,
                                  stop=j == BLOCKS - 1)
                    done.then_inc(o_done, 1)

                pe.wait_ge(proj_copied, 3 * 8)
                logits(0)
                for h in range(HEADS):
                    if h + 1 < HEADS:
                        logits(h + 1)
                    turn_probs(h)
                    if h >= 1:
                        results(h - 1)
                results(HEADS - 1)
                for d in range(CHUNKS):
                    u = u0 + DSA_UNITS - DSA_OUT_UNITS + d // 2
                    if d % 2 == 0:
                        pe.wait_ge(w_lo_made, u + 1)
                    if d >= 2:
                        pe.wait_ge(x_updated, CHUNKS * s + d - 1)
                    for k in range(HEADS):
                        if d == 0:
                            pe.wait_ge(o_lo_made, k + 1)
                        done = product(bank[4 + d % 2][:, :], u % 2, (d % 2 * HEADS + k) * P,
                                       cols(o_hi, k), cols(o_lo, k), k == 0, k == HEADS - 1)
                    done.then_inc(unit_done if d % 2 else half_done, 1)
        sum_over_features(("norm", len(SUBLAYERS)))
        broadcast(("norm", len(SUBLAYERS)))



def rotary_table():
    pairs = RET_DK // 2
    freq = np.float32(1.0) / np.float32(ROT_BASE) ** np.linspace(0.0, 1.0, pairs, dtype=np.float32)
    angle = (np.arange(SEQ, dtype=np.float32)[None, :] * freq.astype(np.float32)[:, None]).astype(np.float32)
    return np.stack([np.cos(angle), np.sin(angle)]).astype(np.float32)


def decay_table():
    log_gamma = np.log(1.0 - 2.0 ** (-5.0 - np.arange(RET_HEADS)))
    ahead = np.arange(SEQ)[None, :] - np.arange(P)[:, None]
    table = np.exp(np.maximum(ahead, 0)[None] * log_gamma[:, None, None]) * (ahead >= 0)[None]
    return (table * RET_DK ** -0.5).astype(np.float32)


def stationary(w):
    rows, columns = w.shape
    return w.reshape(rows // P, P, columns // P, P).transpose(2, 1, 0, 3)


def laid_out(a):
    f32 = {k: np.asarray(v) for k, v in a.items()}
    by_partition = lambda v: v.reshape(-1, P).T

    ffn_in, ffn_out = [], []
    for layer in range(f32["w_ffn1_in"].shape[0]):
        for name in ("w_ffn1", "w_ffn2"):
            t = stationary(f32[name + "_in"][layer])
            ffn_in.append(np.stack([t[:FF_TILES], t[FF_TILES:]], axis=2).reshape(FF_TILES, P, UNIT))
            t = stationary(f32[name + "_out"][layer])
            t = t.reshape(CHUNKS, P, 2, HALF_TILES, P).transpose(0, 2, 1, 3, 4)
            ffn_out.append(t.reshape(FFN_OUT_UNITS, P, OUT_UNIT))

    w = f32["ret_w_in"][0]
    qk, vg = RET_HEADS * RET_DK, RET_HEADS * RET_DV
    ret_in = []
    for h in range(RET_HEADS):
        for at in (0, qk):
            part = w[:, at + h * RET_DK:at + (h + 1) * RET_DK]
            pairs = part.reshape(D_MODEL, RET_DK // 2, 2).transpose(0, 2, 1).reshape(D_MODEL, RET_DK)
            ret_in.append(stationary(pairs).transpose(1, 0, 2, 3).reshape(P, UNIT))
        v = w[:, 2 * qk + h * RET_DV:2 * qk + (h + 1) * RET_DV].reshape(2, CHUNKS // 2, P, RET_DV)
        ret_in += list(v.transpose(0, 2, 1, 3).reshape(2, P, UNIT))
        g = stationary(w[:, 2 * qk + vg + h * RET_DV:2 * qk + vg + (h + 1) * RET_DV])
        ret_in += [g[2 * n:2 * n + 2].transpose(1, 0, 2, 3).reshape(P, UNIT) for n in range(2)]
    ret_out = stationary(f32["ret_w_out"][0]).reshape(CHUNKS, P, UNIT)

    w = f32["dsa_w_in"][0]
    dsa = list(w[:, :2 * RANK].reshape(2, CHUNKS // 2, P, 2 * RANK).transpose(0, 2, 1, 3)
               .reshape(2, P, UNIT))
    for name in ("dsa_w_uq", "dsa_w_uk"):
        dsa.append(stationary(f32[name][0].reshape(RANK, D_MODEL)).transpose(1, 0, 2, 3).reshape(P, UNIT))
    dsa.append(f32["dsa_w_uv"][0].reshape(2, P, D_MODEL).transpose(1, 0, 2).reshape(P, UNIT))
    t = stationary(f32["dsa_w_out"][0])
    dsa += [t[2 * n:2 * n + 2].transpose(1, 0, 2, 3).reshape(P, UNIT) for n in range(DSA_OUT_UNITS)]
    idx = w[:, 2 * RANK:].reshape(CHUNKS, P, IDX_COLS).transpose(1, 0, 2).reshape(P, -1)
    q_idx = f32["dsa_w_qidx"][0].reshape(2, P, IDX_HEADS * IDX_DIM).transpose(1, 0, 2).reshape(P, -1)

    norms = []
    for layer in range(f32["norm_mix"].shape[0]):
        norms += [by_partition(f32[n][layer]) for n in ("norm_ffn1", "norm_mix", "norm_ffn2")]
    norms += [by_partition(f32["final_norm"])]
    norms += [by_partition(f32[n][0]) for n in ("dsa_q_norm", "dsa_kv_norm")]
    norms += [by_partition(np.tile(f32[n][0], 2)) for n in ("dsa_kidx_g", "dsa_kidx_b")]

    x = f32["x"][0]
    return {
        "x_in": x.T.reshape(CHUNKS, P, SEQ).transpose(1, 0, 2).reshape(P, CHUNKS * SEQ),
        "w_ffn_in": np.concatenate(ffn_in),
        "w_ffn_out": np.concatenate(ffn_out),
        "w_ret_in": np.stack(ret_in),
        "w_ret_out": ret_out,
        "w_dsa": np.stack(dsa),
        "w_dsa_idx": np.concatenate([idx, q_idx], axis=1),
        "gains_in": np.concatenate(norms, axis=1),
        "rotary_in": rotary_table(),
        "decay_in": decay_table(),
    }


def kernel(**inputs):
    import concourse.bacc as bacc
    from concourse.bass_utils import run_bass_kernel_spmd

    nc = bacc.Bacc("TRN2", target_bir_lowering=False, num_devices=1)
    arrays = {k: np.ascontiguousarray(v) for k, v in laid_out(inputs).items()}
    args = {k: nc.dram_tensor(k, v.shape, mybir.dt.from_np(v.dtype), kind="ExternalInput").ap()
            for k, v in arrays.items()}
    out = nc.dram_tensor("out", (P, CHUNKS, SEQ), FP32, kind="ExternalOutput").ap()
    hybrid_trunk_kernel(nc, *args.values(), out)
    result = run_bass_kernel_spmd(nc, [arrays], core_ids=[0]).results[0]["out"]
    return np.ascontiguousarray(result.transpose(2, 1, 0).reshape(1, SEQ, D_MODEL))
```

```python
from contextlib import ExitStack

import numpy as np

import concourse.bass as bass
from concourse import mybir

P = 128
D_MODEL, SEQ, D_FF = 1024, 512, 2816
EPS = 1e-6
CHUNKS = D_MODEL // P
BLOCKS = SEQ // P
FF_TILES = D_FF // P
RET_HEADS, RET_DK, RET_DV = 4, 256, 512
ROT_BASE = 10000.0
RET_TILES = RET_HEADS * RET_DV // P
V_TILES = RET_DV // P
HEADS, HEAD_DIM = 8, 128
RANK = 256
IDX_HEADS, IDX_DIM = 8, 64
IDX_COLS = IDX_DIM + IDX_HEADS
TOP_K = min(256, SEQ // 4)
MASKED, TAKEN = -3.0e38, -3.4e38
UNSELECTED = -1.0e37

UNIT = 2048
HALF_TILES = FF_TILES // 2
OUT_UNIT = HALF_TILES * P
FFN_IN_UNITS, FFN_OUT_UNITS = FF_TILES, 2 * CHUNKS
FFN_UNITS = FFN_IN_UNITS + FFN_OUT_UNITS
RET_HEAD_UNITS = 6
RET_IN_UNITS, RET_OUT_UNITS = RET_HEADS * RET_HEAD_UNITS, CHUNKS
DSA_OUT_UNITS = 4
DSA_SIZES = [UNIT, CHUNKS * IDX_COLS, UNIT // 2, UNIT // 2, RANK // P * IDX_HEADS * IDX_DIM] \
    + [UNIT] * (3 + DSA_OUT_UNITS)
DSA_UNITS = len(DSA_SIZES)
assert DSA_UNITS % 2 == 0
SUBLAYERS = ("ffn", "ret", "ffn", "ffn", "dsa", "ffn")
UNITS_OF = {"ffn": FFN_UNITS, "ret": RET_IN_UNITS + RET_OUT_UNITS, "dsa": DSA_UNITS}
FIRST_UNIT = [sum(UNITS_OF[k] for k in SUBLAYERS[:s]) for s in range(len(SUBLAYERS) + 1)]
TILES_OF = {"ffn": FF_TILES, "ret": RET_TILES, "dsa": 0}
FIRST_TILE = [sum(TILES_OF[k] for k in SUBLAYERS[:s]) for s in range(len(SUBLAYERS) + 1)]
STATS = []
for _s, _kind in enumerate(SUBLAYERS):
    STATS.append(("norm", _s))
    if _kind == "ret":
        STATS += [("head", h) for h in range(RET_HEADS)]
STATS.append(("norm", len(SUBLAYERS)))
POOL_CHUNKS = CHUNKS // 2

FP32, FP32R = mybir.dt.float32, mybir.dt.float32r
ALU = mybir.AluOpType
ACT = mybir.ActivationFunctionType


def stat_count(which):
    return STATS.index(which) + 1


def broadcast_count(which):
    dsa = ("norm", SUBLAYERS.index("dsa"))
    return len([w for w in STATS[:stat_count(which)] if w != dsa])


def square_ops(which):
    if which == ("norm", 0):
        return 2 + 2 * POOL_CHUNKS
    if which == ("norm", len(SUBLAYERS)):
        return 1 + 2 * (CHUNKS - 1)
    return {"norm": 1 + 2 * CHUNKS, "head": V_TILES - 1}[which[0]]


def squares_before(which):
    return sum(square_ops(w) for w in STATS[:STATS.index(which)])


def hybrid_trunk_kernel(nc, x_in, w_ffn_in, w_ffn_out, w_ret_in, w_ret_out, w_dsa, w_dsa_idx,
                        gains_in, rotary_in, decay_in, out):
    with ExitStack() as ctx:
        build(nc, ctx, x_in, w_ffn_in, w_ffn_out, w_ret_in, w_ret_out, w_dsa, w_dsa_idx,
              gains_in, rotary_in, decay_in, out)


def build(nc, ctx, x_in, w_ffn_in, w_ffn_out, w_ret_in, w_ret_out, w_dsa, w_dsa_idx,
          gains_in, rotary_in, decay_in, out):
    top = (nc.sbuf_base + 63) // 64 * 64

    def place(name, width, dtype=FP32):
        nonlocal top
        t = nc.alloc_sbuf_tensor_at(name, [P, width], dtype, offset=top)
        top += (4 * width + 31) // 32 * 32
        return t

    x_res = place("x_res", CHUNKS * SEQ)
    xn_hi = place("xn_hi", CHUNKS * SEQ, FP32R)
    xn_lo = place("xn_lo", CHUNKS * SEQ, FP32R)
    w_raw = [place(f"w_raw{n}", UNIT) for n in range(2)]
    w_hi = [place(f"w_hi{n}", UNIT, FP32R) for n in range(2)]
    w_lo = [place(f"w_lo{n}", UNIT, FP32R) for n in range(2)]
    temp = place("temp", 4 * SEQ)
    r_norm = place("r_norm", SEQ)
    square = place("square", SEQ)
    square_sum = place("square_sum", SEQ)
    identity = place("identity", P)
    ones = place("ones", P)
    diagonal = place("diagonal", SEQ)
    GAINS = 7 * CHUNKS + 6
    gains = place("gains", GAINS)
    minus_half = place("minus_half", 16)
    mean_sq = place("mean_sq", BLOCKS)
    r_col = place("r_col", BLOCKS)
    head_r_col = place("head_r_col", BLOCKS)
    arena = top

    gated_hi = place("gated_hi", FF_TILES * SEQ, FP32R)
    gated_lo = place("gated_lo", FF_TILES * SEQ, FP32R)
    rot_cos = place("rot_cos", SEQ)
    rot_sin = place("rot_sin", SEQ)
    decay = place("decay", SEQ)

    top = arena
    ret_hi = place("ret_hi", RET_TILES * SEQ, FP32R)
    ret_lo = place("ret_lo", RET_TILES * SEQ, FP32R)
    q_rot = place("q_rot", 2 * SEQ)
    k_rot = place("k_rot", 2 * SEQ)
    v_tok = place("v_tok", BLOCKS * RET_DV)
    from_key = [sum(SEQ - P * i for i in range(j)) for j in range(BLOCKS + 1)]
    to_query = [sum(P * (i + 1) for i in range(b)) for b in range(BLOCKS + 1)]
    scores = place("scores", from_key[BLOCKS])
    r_head = place("r_head", SEQ)
    assert top <= arena + 8 * FF_TILES * SEQ

    top = arena
    q_heads = place("q_heads", HEADS * SEQ)
    o_hi = nc.alloc_sbuf_tensor_at("o_hi", [P, HEADS * SEQ], FP32R, offset=arena)
    k_heads = place("k_heads", HEADS * SEQ)
    v_at = top
    v_heads = place("v_heads", BLOCKS * D_MODEL)
    latents = nc.alloc_sbuf_tensor_at("latents", [P, 2 * BLOCKS * RANK], FP32, offset=v_at)
    o_lo = nc.alloc_sbuf_tensor_at("o_lo", [P, HEADS * SEQ], FP32R, offset=top)
    latent_hi = [place(f"latent_hi{n}", SEQ, FP32R) for n in range(4)]
    latent_lo = [place(f"latent_lo{n}", SEQ, FP32R) for n in range(4)]
    k_idx = place("k_idx", SEQ)
    q_idx = place("q_idx", IDX_HEADS * IDX_DIM // P * SEQ)
    idx_scores = place("idx_scores", to_query[BLOCKS])
    select_bias = place("select_bias", to_query[BLOCKS])
    probs_t = [place(f"probs_t{n}", SEQ) for n in range(3)]
    k_tok = place("k_tok", BLOCKS * IDX_DIM)
    k_twice = place("k_twice", BLOCKS * P)
    idx_w = place("idx_w", BLOCKS * IDX_HEADS)
    k_mean = place("k_mean", BLOCKS)
    sum_sq = place("sum_sq", 3 * BLOCKS)
    mean_sq3 = place("mean_sq3", 3 * BLOCKS)
    r_col3 = place("r_col3", 3 * BLOCKS)
    best8 = [place(f"best8_{n}", 8) for n in range(2)]
    minus_max = place("minus_max", 4)
    row_sum = place("row_sum", 4)
    row_inv = place("row_inv", 4)

    bank = [ctx.enter_context(nc.psum_tensor(f"bank{n}", [P, SEQ], FP32)) for n in range(8)]

    def sem(name):
        return ctx.enter_context(nc.semaphore(name))

    x_loaded = [sem(f"x_loaded{n}") for n in range(CHUNKS // 2)]
    gains_loaded, rotary_loaded = sem("gains_loaded"), sem("rotary_loaded")
    gate0_loaded = sem("gate0_loaded")
    gate0_hi_made, gate0_lo_made = sem("gate0_hi_made"), sem("gate0_lo_made")
    x_squared, x_squares_added = sem("x_squared"), sem("x_squares_added")
    decay_loaded, decay_reloaded = sem("decay_loaded"), sem("decay_reloaded")
    raw_loaded = [sem(f"raw_loaded{n}") for n in range(2)]
    w_hi_made, w_lo_made = sem("w_hi_made"), sem("w_lo_made")
    unit_done = sem("unit_done")
    half_done = sem("half_done")
    x_updated = sem("x_updated")
    xn_hi_made, xn_lo_made = sem("xn_hi_made"), sem("xn_lo_made")
    squares_done = sem("squares_done")
    stat_done = sem("stat_done")
    mean_done = sem("mean_done")
    r_col_done = sem("r_col_done")
    diagonal_done = sem("diagonal_done")
    broadcast_done = sem("broadcast_done")
    r_ready = sem("r_ready")
    temp_filled = sem("temp_filled")
    silu_done = sem("silu_done")
    gated_done = sem("gated_done")
    gated_hi_made, gated_lo_made = sem("gated_hi_made"), sem("gated_lo_made")
    vector_step = sem("vector_step")
    qk_rotated = sem("qk_rotated")
    v_scaled = sem("v_scaled")
    scores_done, scores_decayed = sem("scores_done"), sem("scores_decayed")
    ret_out_done = sem("ret_out_done")
    ret_squared = sem("ret_squared")
    consts_made = sem("consts_made")
    latents_copied, latents_squared, latents_scaled = (
        sem("latents_copied"), sem("latents_squared"), sem("latents_scaled"))
    k_copied, k_centred, k_squared, k_scaled = (
        sem("k_copied"), sem("k_centred"), sem("k_squared"), sem("k_scaled"))
    mean3_done, r_col3_done = sem("mean3_done"), sem("r_col3_done")
    latents_turned, k_turned = sem("latents_turned"), sem("k_turned")
    latent_hi_made, latent_lo_made, k_idx_made = (
        sem("latent_hi_made"), sem("latent_lo_made"), sem("k_idx_made"))
    q_idx_done, q_idx_copied = sem("q_idx_done"), sem("q_idx_copied")
    dots_done, relu_done, weighted = sem("dots_done"), sem("relu_done"), sem("weighted")
    causal_done, bias_made = sem("causal_done"), sem("bias_made")
    proj_done, proj_copied = sem("proj_done"), sem("proj_copied")
    logits_done, max_done, exp_done, probs_done = (
        sem("logits_done"), sem("max_done"), sem("exp_done"), sem("probs_done"))
    idx_copied, idx_turned = sem("idx_copied"), sem("idx_turned")
    probs_turned, probs_t_copied = sem("probs_turned"), sem("probs_t_copied")
    o_done, o_hi_made, o_lo_made = sem("o_done"), sem("o_hi_made"), sem("o_lo_made")
    last_squared, final_diagonal_done = sem("last_squared"), sem("final_diagonal_done")
    y_done = sem("y_done")
    stored = sem("stored")

    block = ctx.enter_context(nc.Block())

    STAT_BANK = 7
    DSA_BLOCKS = range(TOP_K // P, BLOCKS)
    DOTS = [(b, hh) for b in DSA_BLOCKS for hh in range(IDX_HEADS)]
    DOT_BANKS = (4, 5, 6, 7)
    PROJ_BANKS = (0, 1, 4, 5)
    STEPS = [(b, h) for b in range(BLOCKS) for h in range(HEADS)]
    ROUND_STEPS = range(8, 21)
    EARLY_ROUNDS = TOP_K // 8 - len(ROUND_STEPS)
    POOL_SPLITS = (DSA_UNITS - DSA_OUT_UNITS - 2, DSA_UNITS - DSA_OUT_UNITS + 2)
    FIRST_LOGITS, FIRST_COPIED = (3 * 8 - 2, 3 * 8 - 1), 3 * 8 - 4
    Q_IDX_TILES = IDX_HEADS * IDX_DIM // P

    def first_rounds(c):
        return IDX_HEADS < c < len(DOTS)

    def cols(t, i, width=SEQ):
        return t[:, bass.ts(i, width)]

    def tile(t, i):
        return t[:, i * P:(i + 1) * P]

    def unit_size(u):
        for s, kind in enumerate(SUBLAYERS):
            n = u - FIRST_UNIT[s]
            if n < UNITS_OF[kind]:
                if kind == "ffn" and n >= FFN_IN_UNITS:
                    return OUT_UNIT
                return DSA_SIZES[n] if kind == "dsa" else UNIT

    def gain(norm, k):
        return gains[:, bass.ds(norm * CHUNKS + k, 1)]

    def squares_of(e):
        return cols((q_rot, k_rot)[e // 2], e % 2)

    def latent_bank(n):
        return bank[(5, 6, 2, 3)[n]]

    def scores_of(b):
        return idx_scores[:, to_query[b]:to_query[b + 1]]

    def step_bufs(i):
        keys = P * (STEPS[i][0] + 1)
        return (keys, bank[(2, 0, 1)[i % 3]][:, :keys], cols(temp, i % 4)[:, :keys],
                bank[3 + i % 2][:, :keys], probs_t[i % 3][:, :keys], slice(i % 4, i % 4 + 1))

    def four_heads(t, q):
        part = t[:, :].rearrange("p (h t) -> p h t", h=HEADS)
        return part[:, 4 * (q % 2):4 * (q % 2) + 4, P * (q // 2):P * (q // 2 + 1)]

    def results_bank(q):
        return bank[5 + q % 3]

    @block.sync
    def _(sp):
        def load(u, source, pair=0):
            if u >= 2:
                sp.wait_ge(w_lo_made, u - 1 + 2 * pair)
            sp.dma_start(w_raw[u % 2][:, :source.shape[-1]], source).then_inc(raw_loaded[u % 2], 16)

        for s, kind in enumerate(SUBLAYERS):
            u0 = FIRST_UNIT[s]
            if kind == "ffn":
                f = SUBLAYERS[:s].count("ffn")
                first = 0
                if s == 0:
                    half = UNIT // 2
                    sp.dma_start(w_raw[0][:, :half], w_ffn_in[0][:, :half]).then_inc(gate0_loaded, 16)
                    sp.dma_start(gains[:, :], gains_in).then_inc(gains_loaded, 16)
                    for k in range(0, CHUNKS, 2):
                        sp.dma_start(x_res[:, k * SEQ:(k + 2) * SEQ], x_in[:, k * SEQ:(k + 2) * SEQ])\
                            .then_inc(x_loaded[k // 2], 16)
                    sp.dma_start(w_raw[0][:, half:], w_ffn_in[0][:, half:]).then_inc(raw_loaded[0], 16)
                    load(1, w_ffn_in[1])
                    sp.dma_start(rot_cos[:, :], rotary_in[0]).then_inc(rotary_loaded, 16)
                    sp.dma_start(rot_sin[:, :], rotary_in[1]).then_inc(rotary_loaded, 16)
                    sp.dma_start(decay[:, :], decay_in[0]).then_inc(decay_loaded, 16)
                    first = 1
                with sp.Fori(0, FFN_IN_UNITS // 2 - first) as i:
                    for n in range(2):
                        load(u0 + 2 * first + n, w_ffn_in[2 * i + (f * FFN_IN_UNITS + 2 * first + n)], i)
                with sp.Fori(0, FFN_OUT_UNITS // 2) as i:
                    for n in range(2):
                        load(u0 + FFN_IN_UNITS + n, w_ffn_out[2 * i + (f * FFN_OUT_UNITS + n)], i)
            elif kind == "ret":
                with sp.Fori(0, RET_IN_UNITS // 2) as i:
                    for n in range(2):
                        load(u0 + n, w_ret_in[2 * i + n], i)
                with sp.Fori(0, RET_OUT_UNITS // 2) as i:
                    for n in range(2):
                        load(u0 + RET_IN_UNITS + n, w_ret_out[2 * i + n], i)
            else:
                half, idx = UNIT // 2, DSA_SIZES[1]
                sources = [w_dsa[0], w_dsa_idx[:, :idx], w_dsa[1][:, :half], w_dsa[1][:, half:],
                           w_dsa_idx[:, idx:]] + [w_dsa[n] for n in range(2, 5 + DSA_OUT_UNITS)]
                for n, source in enumerate(sources):
                    load(u0 + n, source)
        for k in range(CHUNKS):
            sp.wait_ge(y_done, k + 1)
            sp.dma_start(out[:, k, :], cols(x_res, k)).then_inc(stored, 16)
        sp.wait_ge(stored, 16 * CHUNKS)

    @block.gpsimd
    def _(pool):
        nc.gpsimd.memset(minus_half[:, :], -0.5).then_inc(consts_made, 1)
        nc.gpsimd.memset(ones[:, :], 1.0).then_inc(consts_made, 1)
        nc.gpsimd.memset(identity[:, :], 0.0).then_inc(consts_made, 1)
        pool.wait_ge(consts_made, 3)
        nc.gpsimd.affine_select(out=identity[:, :], in_=identity[:, :], compare_op=ALU.not_equal,
                                fill=1.0, base=0, pattern=[[-1, P]],
                                channel_multiplier=1).then_inc(consts_made, 1)

        def sum_norm_squares(s, chunk_ready):
            before = squares_before(("norm", s))
            nc.gpsimd.memset(square_sum[:, :], 0.0).then_inc(squares_done, 1)

            def chunk(k):
                chunk_ready(k)
                pool.wait_ge(squares_done, 2 * k + (before + 1))
                nc.gpsimd.tensor_tensor(square[:, :], cols(x_res, k), cols(x_res, k), ALU.mult)\
                    .then_inc(squares_done, 1)
                pool.wait_ge(squares_done, 2 * k + (before + 2))
                nc.gpsimd.tensor_tensor(square_sum[:, :], square_sum[:, :], square[:, :], ALU.add)\
                    .then_inc(squares_done, 1)

            if s == 0:
                for k in range(POOL_CHUNKS):
                    chunk(k)
                pool.wait_ge(x_squares_added, 2)
                pool.wait_ge(squares_done, before + 1 + 2 * POOL_CHUNKS)
                nc.gpsimd.tensor_tensor(square_sum[:, :], square_sum[:, :], cols(temp, 0), ALU.add)\
                    .then_inc(squares_done, 1)
            else:
                with pool.Fori(0, CHUNKS - int(s == len(SUBLAYERS))) as k:
                    chunk(k)

        def inverse_rms(which, to):
            pool.wait_ge(mean_done, stat_count(which))
            nc.gpsimd.tensor_tensor(to[:, :], mean_sq[:, :], minus_half[:, :BLOCKS], ALU.pow)\
                .then_inc(r_col_done, 1)

        sum_norm_squares(0, lambda k: pool.wait_ge(x_loaded[k // 2], 16))
        for s, kind in enumerate(SUBLAYERS):
            u0 = FIRST_UNIT[s]
            inverse_rms(("norm", s), r_col)
            if kind == "ret":
                for h in range(RET_HEADS):
                    before = squares_before(("head", h))
                    pool.wait_ge(ret_squared, V_TILES * h + 2)
                    nc.gpsimd.tensor_tensor(square_sum[:, :], squares_of(0), squares_of(1), ALU.add)\
                        .then_inc(squares_done, 1)
                    for e in range(2, V_TILES):
                        pool.wait_ge(ret_squared, V_TILES * h + e + 1)
                        pool.wait_ge(squares_done, before + e - 1)
                        nc.gpsimd.tensor_tensor(square_sum[:, :], square_sum[:, :], squares_of(e),
                                                ALU.add).then_inc(squares_done, 1)
                    if h + 1 < RET_HEADS:
                        pool.wait_ge(scores_decayed, BLOCKS * (h + 1))
                        pool.dma_start(decay[:, :], decay_in[h + 1]).then_inc(decay_reloaded, 16)
                    inverse_rms(("head", h), head_r_col)
            if kind == "dsa":
                def split_unit(u):
                    pool.wait_ge(w_hi_made, u + 1)
                    pool.wait_ge(w_lo_made, u)
                    nc.gpsimd.tensor_tensor(w_lo[u % 2][:, :], w_raw[u % 2][:, :],
                                            w_hi[u % 2][:, :].bitcast(FP32), ALU.subtract)\
                        .then_inc(w_lo_made, 1)

                for n, part in enumerate((slice(0, 2 * BLOCKS), slice(2 * BLOCKS, 3 * BLOCKS))):
                    pool.wait_ge(mean3_done, n + 2)
                    nc.gpsimd.tensor_tensor(r_col3[:, part], mean_sq3[:, part], minus_half[:, part],
                                            ALU.pow).then_inc(r_col3_done, 1)
                nc.gpsimd.memset(select_bias[:, :P], 0.0).then_inc(causal_done, 1)
                pool.wait_ge(causal_done, 1)
                nc.gpsimd.affine_select(out=select_bias[:, :P], in_=select_bias[:, :P],
                                        compare_op=ALU.is_ge, fill=UNSELECTED, base=0,
                                        pattern=[[-1, P]], channel_multiplier=1)\
                    .then_inc(causal_done, 1)
                for n, b in enumerate(DSA_BLOCKS):
                    pool.wait_ge(weighted, IDX_HEADS * (n + 1))
                    own = idx_scores[:, to_query[b + 1] - P:to_query[b + 1]]
                    nc.gpsimd.affine_select(out=own, in_=own, compare_op=ALU.is_ge, fill=MASKED,
                                            base=0, pattern=[[-1, P]], channel_multiplier=1)\
                        .then_inc(causal_done, 1)
                    if n == 0:
                        split_unit(u0 + POOL_SPLITS[0])
                for u in range(u0 + POOL_SPLITS[0] + 1, u0 + POOL_SPLITS[1]):
                    split_unit(u)
            sum_norm_squares(s + 1, lambda k: pool.wait_ge(x_updated, k + (CHUNKS * s + 1)))
        inverse_rms(("norm", len(SUBLAYERS)), r_col)

    @block.scalar
    def _(act):
        copy = ACT.Copy

        def split_unit(u, pair=0):
            size = unit_size(u)
            act.wait_ge(raw_loaded[u % 2], 16 * (u // 2 + 1) + 16 * pair)
            if u >= 2:
                act.wait_ge(unit_done, u - 1 + 2 * pair)
            nc.scalar.activation(w_hi[u % 2][:, :size], w_raw[u % 2][:, :size], copy)\
                .then_inc(w_hi_made, 1)

        def stream_hi(norm, k):
            nc.scalar.activation(cols(xn_hi, k), cols(x_res, k), copy, scale=gain(norm, k))\
                .then_inc(xn_hi_made, 1)

        def copy_broadcast(which, to):
            act.wait_ge(broadcast_done, broadcast_count(which))
            nc.scalar.activation(to[:, :], bank[STAT_BANK][:, :], copy).then_inc(r_ready, 1)

        def gated_tile(count, slot, hi, index):
            gate = cols(temp, 2 * slot)
            act.wait_ge(temp_filled, count)
            nc.scalar.activation(gate, gate, ACT.Silu).then_inc(silu_done, 1)
            act.wait_ge(gated_done, count)
            nc.scalar.activation(cols(hi, index), gate, copy).then_inc(gated_hi_made, 1)

        def residual(s, d):
            act.wait_ge(x_updated, CHUNKS * s + 1 + d)
            stream_hi(s + 1, d)

        half = UNIT // 2
        act.wait_ge(consts_made, 1)
        nc.scalar.activation(head_r_col[:, :], minus_half[:, :4], copy)
        act.wait_ge(gate0_loaded, 16)
        nc.scalar.activation(w_hi[0][:, :half], w_raw[0][:, :half], copy).then_inc(gate0_hi_made, 1)
        act.wait_ge(gains_loaded, 16)
        for k in range(CHUNKS):
            if k % 2 == 0:
                act.wait_ge(x_loaded[k // 2], 16)
            stream_hi(0, k)
        act.wait_ge(raw_loaded[0], 16)
        nc.scalar.activation(w_hi[0][:, half:], w_raw[0][:, half:], copy).then_inc(w_hi_made, 1)
        for k in range(POOL_CHUNKS, CHUNKS):
            nc.scalar.activation(cols(temp, k - POOL_CHUNKS), cols(x_res, k), ACT.Square)\
                .then_inc(x_squared, 1)
        split_unit(1)

        for s, kind in enumerate(SUBLAYERS):
            u0, tile0 = FIRST_UNIT[s], FIRST_TILE[s]
            last = s == len(SUBLAYERS) - 1
            if kind == "ffn":
                def in_pair(first, pair):
                    for n in range(2):
                        step = 2 * first + n
                        split_unit(u0 + step + 2, pair)
                        if step == 0:
                            copy_broadcast(("norm", s), r_norm)
                        gated_tile(tile0 + step + 1 + 2 * pair, n, gated_hi, step + 2 * pair)

                in_pair(0, 0)
                with act.Fori(0, FFN_IN_UNITS // 2 - 2) as i:
                    in_pair(1, i)
                in_pair(FFN_IN_UNITS // 2 - 1, 0)

                def out_tile(first, i):
                    for n in range(2):
                        if last and first == CHUNKS - 1:
                            continue
                        split_unit(u0 + FFN_IN_UNITS + 2 * first + n + 2, i)
                    if not last:
                        residual(s, first + i)

                with act.Fori(0, CHUNKS - 1) as i:
                    out_tile(0, i)
                out_tile(CHUNKS - 1, 0)
            elif kind == "ret":
                for h in range(RET_HEADS):
                    u = u0 + RET_HEAD_UNITS * h
                    if h == 0:
                        split_unit(u + 2)
                        copy_broadcast(("norm", s), r_norm)
                    else:
                        split_unit(u + 2)
                    split_unit(u + 3)
                    split_unit(u + 4)
                    act.wait_ge(unit_done, u + 4)
                    for b in range(BLOCKS):
                        nc.scalar.activation(cols(v_tok, b), bank[b][:, :], copy,
                                             scale=r_col[:, b:b + 1]).then_inc(v_scaled, 1)
                    split_unit(u + 5)
                    for e in range(V_TILES):
                        act.wait_ge(ret_out_done, V_TILES * h + e + 1)
                        nc.scalar.activation(squares_of(e), bank[e][:, :], ACT.Square)\
                            .then_inc(ret_squared, 1)

                    def silu(e):
                        act.wait_ge(temp_filled, tile0 + V_TILES * h + e + 1)
                        nc.scalar.activation(cols(temp, e), cols(temp, e), ACT.Silu)\
                            .then_inc(silu_done, 1)

                    def result_hi(e):
                        n = V_TILES * h + e
                        act.wait_ge(gated_done, tile0 + n + 1)
                        nc.scalar.activation(cols(ret_hi, n), cols(temp, e), copy)\
                            .then_inc(gated_hi_made, 1)

                    silu(0)
                    silu(1)
                    copy_broadcast(("head", h), r_head)
                    split_unit(u + 6)
                    result_hi(0)
                    result_hi(1)
                    silu(2)
                    result_hi(2)
                    silu(3)
                    split_unit(u + 7)
                    result_hi(3)
                with act.Fori(0, CHUNKS // 2 - 1) as i:
                    for n in range(2):
                        split_unit(u0 + RET_IN_UNITS + 2 + n, i)
                        residual(s, 2 * i + n)
                for n in range(2):
                    split_unit(FIRST_UNIT[s + 1] + n)
                    residual(s, CHUNKS - 2 + n)
            else:
                def copy_latents(part):
                    for b in range(BLOCKS):
                        nc.scalar.activation(cols(latents, part * BLOCKS + b, RANK),
                                             bank[b][:, part * RANK:(part + 1) * RANK], copy,
                                             scale=r_col[:, b:b + 1]).then_inc(latents_copied, 1)

                def square_latents(part):
                    act.wait_ge(latents_copied, (part + 1) * BLOCKS)
                    for b in range(BLOCKS):
                        n, at = part * BLOCKS + b, 2 * part * BLOCKS + b
                        nc.scalar.activation(cols(temp, n, RANK), cols(latents, n, RANK), ACT.Square,
                                             accum_out=sum_sq[:, at:at + 1]).then_inc(latents_squared, 1)

                def latent_parts(part):
                    for n in (2 * part, 2 * part + 1):
                        act.wait_ge(latents_turned, n + 1)
                        nc.scalar.activation(latent_hi[n][:, :], latent_bank(n)[:, :], copy,
                                             scale=gains[:, 7 * CHUNKS + n:7 * CHUNKS + n + 1])\
                            .then_inc(latent_hi_made, 1)

                act.wait_ge(r_col_done, stat_count(("norm", s)))
                act.wait_ge(unit_done, u0 + 1)
                split_unit(u0 + 2)
                copy_latents(0)
                act.wait_ge(unit_done, u0 + 2)
                nc.scalar.activation(r_norm[:IDX_COLS, :], bank[5][:IDX_COLS, :], copy)\
                    .then_inc(idx_copied, 1)
                split_unit(u0 + 3)
                act.wait_ge(idx_turned, 1)
                for b in range(BLOCKS):
                    nc.scalar.activation(cols(k_tok, b, IDX_DIM),
                                         bank[4][:, b * IDX_COLS:b * IDX_COLS + IDX_DIM], copy,
                                         scale=r_col[:, b:b + 1], accum_out=k_mean[:, b:b + 1])\
                        .then_inc(k_copied, 1)
                square_latents(0)
                act.wait_ge(k_centred, BLOCKS)
                for b in range(BLOCKS):
                    nc.scalar.activation(cols(diagonal, b, IDX_DIM), cols(k_tok, b, IDX_DIM), ACT.Square,
                                         accum_out=sum_sq[:, BLOCKS + b:BLOCKS + b + 1])\
                        .then_inc(k_squared, 1)
                split_unit(u0 + 4)
                latent_parts(0)
                act.wait_ge(unit_done, u0 + 4)
                copy_latents(1)
                split_unit(u0 + 5)
                square_latents(1)
                for m in range(Q_IDX_TILES):
                    if m < Q_IDX_TILES - 1:
                        act.wait_ge(q_idx_done, m + 1)
                    else:
                        act.wait_ge(unit_done, u0 + 5)
                    nc.scalar.activation(cols(q_idx, m), bank[DOT_BANKS[m]][:, :], copy)\
                        .then_inc(q_idx_copied, 1)
                for c, (b, hh) in enumerate(DOTS):
                    keys = P * (b + 1)
                    act.wait_ge(dots_done, c + 1)
                    if c >= 4:
                        act.wait_ge(weighted, c - 3)
                    nc.scalar.activation(cols(temp, c % 4)[:, :keys], bank[DOT_BANKS[c % 4]][:, :keys],
                                         ACT.Relu, scale=IDX_DIM ** -0.5).then_inc(relu_done, 1)
                    if c == IDX_HEADS:
                        split_unit(u0 + 6)
                latent_parts(1)
                def exps(i):
                    _, _, probs, _, _, at = step_bufs(i)
                    act.wait_ge(max_done, i + 1)
                    nc.scalar.activation(probs, probs, ACT.Exp, bias=minus_max[:, at], scale=-1.0,
                                         accum_out=row_sum[:, at]).then_inc(exp_done, 1)

                for j in range(3 * 8):
                    if j % 8 < 7:
                        act.wait_ge(proj_done, 7 * (j // 8) + j % 8 + 1)
                    else:
                        act.wait_ge(unit_done, u0 + 6 + j // 8)
                    to = (q_heads, k_heads, v_heads)[j // 8]
                    nc.scalar.activation(cols(to, j % 8), bank[PROJ_BANKS[j % 4]][:, :], copy)\
                        .then_inc(proj_copied, 1)
                    if j % 8 == 7 and j < 23:
                        split_unit(u0 + 7 + j // 8)
                    if j >= 22:
                        exps(j - 22)

                def copy_probs_t(i):
                    _, _, _, turned, to, _ = step_bufs(i)
                    act.wait_ge(probs_turned, i + 1)
                    if i >= 3:
                        act.wait_ge(o_done, i - 2)
                    nc.scalar.activation(to, turned, copy).then_inc(probs_t_copied, 1)

                def result_hi(q):
                    act.wait_ge(o_done, 4 * (q + 1))
                    nc.scalar.activation(four_heads(o_hi, q),
                                         results_bank(q)[:, :].rearrange("p (h t) -> p h t", h=4), copy)\
                        .then_inc(o_hi_made, 1)

                for i in range(len(STEPS)):
                    if i == HEADS:
                        split_unit(u0 + 9)
                    copy_probs_t(i)
                    if i + 2 < len(STEPS):
                        exps(i + 2)
                    if i % 4 == 1 and i > 4:
                        result_hi(i // 4 - 1)
                result_hi(len(STEPS) // 4 - 1)
                for d in range(CHUNKS):
                    if d % 2 == 1:
                        split_unit(u0 + DSA_UNITS - DSA_OUT_UNITS + 2 + d // 2)
                    residual(s, d)
        act.wait_ge(x_updated, CHUNKS * len(SUBLAYERS))
        nc.scalar.activation(cols(temp, 0), cols(x_res, CHUNKS - 1), ACT.Square)\
            .then_inc(last_squared, 1)

    @block.vector
    def _(dve):
        steps = [0]

        def count_step(instruction):
            steps[0] += 1
            instruction.then_inc(vector_step, 1)
            return steps[0]

        def link(instruction):
            dve.wait_ge(vector_step, count_step(instruction))

        def split_unit(u, pair=0):
            size = unit_size(u)
            dve.wait_ge(w_hi_made, u + 1 + 2 * pair)
            nc.vector.tensor_tensor(w_lo[u % 2][:, :size], w_raw[u % 2][:, :size],
                                    w_hi[u % 2][:, :size].bitcast(FP32), ALU.subtract)\
                .then_inc(w_lo_made, 1)

        def stream_lo(norm, k):
            dve.wait_ge(xn_hi_made, CHUNKS * norm + 1 + k)
            nc.vector.scalar_tensor_tensor(cols(xn_lo, k), cols(x_res, k), gain(norm, k),
                                           cols(xn_hi, k).bitcast(FP32), ALU.mult, ALU.subtract)\
                .then_inc(xn_lo_made, 1)

        def mean_square(which, width):
            dve.wait_ge(stat_done, stat_count(which))
            nc.vector.tensor_scalar(mean_sq[:, :], bank[STAT_BANK][:, :BLOCKS], 1.0 / width, EPS,
                                    ALU.mult, ALU.add).then_inc(mean_done, 1)

        def spread(which, r):
            dve.wait_ge(r_col_done, stat_count(which))
            for b in range(BLOCKS):
                last = nc.vector.tensor_scalar(tile(diagonal, b), identity[:, :], r[:, b:b + 1], None,
                                               ALU.mult)
            last.then_inc(diagonal_done, 1)

        def fill_temp(slot, gate, value, factor):
            nc.vector.tensor_tensor(cols(temp, 2 * slot), gate[:, :], r_norm[:, :], ALU.mult)
            nc.vector.tensor_tensor(cols(temp, 2 * slot + 1), value[:, :], factor[:, :], ALU.mult)\
                .then_inc(temp_filled, 1)

        def gated_tile(count, slot, hi, lo, index):
            gate = cols(temp, 2 * slot)
            dve.wait_ge(silu_done, count)
            nc.vector.tensor_tensor(gate, gate, cols(temp, 2 * slot + 1), ALU.mult)\
                .then_inc(gated_done, 1)
            dve.wait_ge(gated_hi_made, count)
            nc.vector.tensor_tensor(cols(lo, index), gate, cols(hi, index).bitcast(FP32),
                                    ALU.subtract).then_inc(gated_lo_made, 1)

        def update(s, d, n, factor):
            nc.vector.scalar_tensor_tensor(cols(x_res, d), bank[4 + n][:, :], factor, cols(x_res, d),
                                           ALU.mult, ALU.add).then_inc(x_updated, 1)

        dve.wait_ge(gains_loaded, 16)
        half = UNIT // 2
        dve.wait_ge(gate0_hi_made, 1)
        nc.vector.tensor_tensor(w_lo[0][:, :half], w_raw[0][:, :half],
                                w_hi[0][:, :half].bitcast(FP32), ALU.subtract)\
            .then_inc(gate0_lo_made, 1)
        for k in range(CHUNKS):
            stream_lo(0, k)
        dve.wait_ge(w_hi_made, 1)
        nc.vector.tensor_tensor(w_lo[0][:, half:], w_raw[0][:, half:], w_hi[0][:, half:].bitcast(FP32),
                                ALU.subtract).then_inc(w_lo_made, 1)
        dve.wait_ge(x_squared, 2)
        nc.vector.tensor_tensor(cols(temp, 0), cols(temp, 0), cols(temp, 1), ALU.add)
        dve.wait_ge(x_squared, 4)
        link(nc.vector.tensor_tensor(cols(temp, 2), cols(temp, 2), cols(temp, 3), ALU.add))
        nc.vector.tensor_tensor(cols(temp, 0), cols(temp, 0), cols(temp, 2), ALU.add)\
            .then_inc(x_squares_added, 2)
        split_unit(1)
        dve.wait_ge(consts_made, 4)

        for s, kind in enumerate(SUBLAYERS):
            u0, tile0 = FIRST_UNIT[s], FIRST_TILE[s]
            last = s == len(SUBLAYERS) - 1
            if kind != "dsa":
                mean_square(("norm", s), D_MODEL)
                spread(("norm", s), r_col)
            if kind == "ffn":
                def in_pair(first, pair):
                    for n in range(2):
                        step = 2 * first + n
                        if step == 0:
                            dve.wait_ge(r_ready, broadcast_count(("norm", s)))
                        dve.wait_ge(unit_done, u0 + step + 1 + 2 * pair)
                        fill_temp(n, bank[2 * n], bank[2 * n + 1], r_norm)
                        split_unit(u0 + step + 2, pair)
                        gated_tile(tile0 + step + 1 + 2 * pair, n, gated_hi, gated_lo, step + 2 * pair)

                in_pair(0, 0)
                with dve.Fori(0, FFN_IN_UNITS // 2 - 2) as i:
                    in_pair(1, i)
                in_pair(FFN_IN_UNITS // 2 - 1, 0)

                def out_tile(d, n, pair):
                    u = u0 + FFN_IN_UNITS + 2 * d
                    at_end = last and d == CHUNKS - 1
                    if not at_end:
                        split_unit(u + 2, pair)
                    dve.wait_ge(unit_done, u + 2 + 2 * pair)
                    update(s, d + pair, n, 0.5)
                    if not at_end:
                        split_unit(u + 3, pair)
                    if not last:
                        stream_lo(s + 1, d + pair)

                with dve.Fori(0, CHUNKS // 2 - 1) as i:
                    for n in range(2):
                        out_tile(n, n, 2 * i)
                for n in range(2):
                    out_tile(CHUNKS - 2 + n, n, 0)
            elif kind == "ret":
                dve.wait_ge(r_ready, broadcast_count(("norm", s)))
                dve.wait_ge(rotary_loaded, 32)
                nc.vector.tensor_tensor(rot_cos[:, :], rot_cos[:, :], r_norm[:, :], ALU.mult)
                link(nc.vector.tensor_tensor(rot_sin[:, :], rot_sin[:, :], r_norm[:, :], ALU.mult))

                def rotate(to, even, odd):
                    for n, (a, b, op) in enumerate(((even, odd, ALU.subtract), (odd, even, ALU.add))):
                        nc.vector.tensor_tensor(cols(temp, 2 * n), a[:, :], rot_cos[:, :], ALU.mult)
                        link(nc.vector.tensor_tensor(cols(temp, 2 * n + 1), b[:, :], rot_sin[:, :],
                                                     ALU.mult))
                        done = nc.vector.tensor_tensor(cols(to, n), cols(temp, 2 * n),
                                                       cols(temp, 2 * n + 1), op)
                    done.then_inc(qk_rotated, 1)

                for h in range(RET_HEADS):
                    u = u0 + RET_HEAD_UNITS * h
                    for n, to in enumerate((q_rot, k_rot)):
                        split_unit(u + 2 + n)
                        dve.wait_ge(unit_done, u + 1 + n)
                        rotate(to, bank[4 + 2 * n], bank[5 + 2 * n])
                    split_unit(u + 4)
                    if h == 0:
                        dve.wait_ge(decay_loaded, 16)
                    else:
                        dve.wait_ge(decay_reloaded, 16 * h)
                    for j in range(BLOCKS):
                        width = SEQ - P * j
                        dve.wait_ge(scores_done, BLOCKS * h + j + 1)
                        nc.vector.tensor_tensor(scores[:, from_key[j]:from_key[j + 1]],
                                                bank[4 + j][:, :width], decay[:, :width], ALU.mult)\
                            .then_inc(scores_decayed, 1)
                    split_unit(u + 5)

                    def scale_gate(e):
                        if e % 2 == 0:
                            dve.wait_ge(half_done, 2 * h + e // 2 + 1)
                        else:
                            dve.wait_ge(unit_done, u + 5 + e // 2)
                        nc.vector.tensor_tensor(cols(temp, e), bank[4 + e][:, :], r_norm[:, :], ALU.mult)\
                            .then_inc(temp_filled, 1)

                    def gate_result(e):
                        dve.wait_ge(silu_done, tile0 + V_TILES * h + e + 1)
                        steps[0] += 1
                        nc.vector.tensor_tensor(cols(temp, e), cols(temp, e), bank[e][:, :], ALU.mult)\
                            .then_inc(vector_step, 1)
                        return steps[0]

                    def norm_result(e, gated):
                        n = V_TILES * h + e
                        dve.wait_ge(vector_step, gated)
                        nc.vector.tensor_tensor(cols(temp, e), cols(temp, e), r_head[:, :], ALU.mult)\
                            .then_inc(gated_done, 1)
                        dve.wait_ge(gated_hi_made, tile0 + n + 1)
                        nc.vector.tensor_tensor(cols(ret_lo, n), cols(temp, e),
                                                cols(ret_hi, n).bitcast(FP32), ALU.subtract)\
                            .then_inc(gated_lo_made, 1)

                    scale_gate(0)
                    mean_square(("head", h), RET_DV)
                    gated0 = gate_result(0)
                    spread(("head", h), head_r_col)
                    scale_gate(1)
                    gated1 = gate_result(1)
                    split_unit(u + 6)
                    dve.wait_ge(r_ready, broadcast_count(("head", h)))
                    norm_result(0, gated0)
                    norm_result(1, gated1)
                    scale_gate(2)
                    norm_result(2, gate_result(2))
                    scale_gate(3)
                    gated3 = gate_result(3)
                    split_unit(u + 7)
                    norm_result(3, gated3)

                def out_tile(d, n, pair):
                    u = u0 + RET_IN_UNITS + d
                    dve.wait_ge(unit_done, u + 1 + 2 * pair)
                    update(s, d + 2 * pair, n, 1.0)
                    split_unit(u + 2, pair)
                    stream_lo(s + 1, d + 2 * pair)

                with dve.Fori(0, CHUNKS // 2 - 1) as i:
                    for n in range(2):
                        out_tile(n, n, i)
                for n in range(2):
                    out_tile(CHUNKS - 2 + n, n, 0)
            else:
                def mean_squares(part, width):
                    nc.vector.tensor_scalar(mean_sq3[:, part * BLOCKS:(part + 1) * BLOCKS],
                                            sum_sq[:, part * BLOCKS:(part + 1) * BLOCKS], 1.0 / width,
                                            EPS, ALU.mult, ALU.add).then_inc(mean3_done, 1)

                def scale_latents(part):
                    for b in range(BLOCKS):
                        at = 2 * part * BLOCKS + b
                        to = cols(latents, part * BLOCKS + b, RANK)
                        nc.vector.tensor_scalar(to, to, r_col3[:, at:at + 1], None, ALU.mult)\
                            .then_inc(latents_scaled, 1)

                def latent_parts(part):
                    for n in (2 * part, 2 * part + 1):
                        dve.wait_ge(latent_hi_made, n + 1)
                        nc.vector.scalar_tensor_tensor(latent_lo[n][:, :], latent_bank(n)[:, :],
                                                       gains[:, 7 * CHUNKS + n:7 * CHUNKS + n + 1],
                                                       latent_hi[n][:, :].bitcast(FP32), ALU.mult,
                                                       ALU.subtract).then_inc(latent_lo_made, 1)

                found, marked = {}, {}

                def find_8(b):
                    if b in marked:
                        dve.wait_ge(vector_step, marked[b])
                    found[b] = count_step(nc.vector.max(best8[b % 2][:, :], scores_of(b)))

                def mark_8(b):
                    dve.wait_ge(vector_step, found[b])
                    marked[b] = count_step(nc.vector.match_replace(scores_of(b), best8[b % 2][:, :],
                                                                   scores_of(b), TAKEN))

                def choice_to_bias(b):
                    dve.wait_ge(vector_step, marked[b])
                    nc.vector.tensor_scalar(select_bias[:, to_query[b]:to_query[b + 1]], scores_of(b),
                                            (MASKED + TAKEN) / 2, UNSELECTED, ALU.is_gt, ALU.mult)\
                        .then_inc(bias_made, 1)

                mean_square(("norm", s), D_MODEL)
                split_unit(u0 + 2)
                split_unit(u0 + 3)
                dve.wait_ge(r_col_done, stat_count(("norm", s)))
                dve.wait_ge(k_copied, BLOCKS)
                link(nc.vector.tensor_scalar(k_mean[:, :], k_mean[:, :], 1.0 / IDX_DIM, None, ALU.mult))
                for b in range(BLOCKS):
                    nc.vector.tensor_scalar(cols(k_tok, b, IDX_DIM), cols(k_tok, b, IDX_DIM),
                                            k_mean[:, b:b + 1], None, ALU.subtract)\
                        .then_inc(k_centred, 1)
                for b in range(BLOCKS):
                    nc.vector.tensor_scalar(cols(idx_w, b, IDX_HEADS),
                                            bank[4][:, b * IDX_COLS + IDX_DIM:(b + 1) * IDX_COLS],
                                            r_col[:, b:b + 1], IDX_HEADS ** -0.5, ALU.mult, ALU.mult)
                dve.wait_ge(latents_squared, BLOCKS)
                mean_squares(0, RANK)
                dve.wait_ge(k_squared, BLOCKS)
                mean_squares(1, IDX_DIM)
                dve.wait_ge(r_col3_done, 1)
                scale_latents(0)
                for b in range(BLOCKS):
                    for n in range(2):
                        nc.vector.tensor_scalar(cols(k_twice, 2 * b + n, IDX_DIM), cols(k_tok, b, IDX_DIM),
                                                r_col3[:, BLOCKS + b:BLOCKS + b + 1], None,
                                                ALU.mult).then_inc(k_scaled, 1)
                split_unit(u0 + 4)
                latent_parts(0)
                dve.wait_ge(k_turned, 1)
                nc.vector.tensor_scalar(k_idx[:, :], bank[7][:, :], gains[:, 7 * CHUNKS + 4:7 * CHUNKS + 5],
                                        gains[:, 7 * CHUNKS + 5:7 * CHUNKS + 6], ALU.mult, ALU.add)\
                    .then_inc(k_idx_made, 1)
                split_unit(u0 + 5)
                dve.wait_ge(latents_squared, 2 * BLOCKS)
                mean_squares(2, RANK)
                for c, (b, hh) in enumerate(DOTS):
                    part = cols(temp, c % 4)[:, :P * (b + 1)]
                    head_w = idx_w[:, b * IDX_HEADS + hh:b * IDX_HEADS + hh + 1]
                    if first_rounds(c):
                        find_8(DSA_BLOCKS[0])
                    dve.wait_ge(relu_done, c + 1)
                    if hh == 0:
                        nc.vector.tensor_scalar(scores_of(b), part, head_w, None, ALU.mult)\
                            .then_inc(weighted, 1)
                    else:
                        dve.wait_ge(weighted, c)
                        nc.vector.scalar_tensor_tensor(scores_of(b), part, head_w, scores_of(b),
                                                       ALU.mult, ALU.add).then_inc(weighted, 1)
                    if c == IDX_HEADS - 1:
                        dve.wait_ge(r_col3_done, 2)
                        scale_latents(1)
                    if c == IDX_HEADS:
                        dve.wait_ge(causal_done, 3)
                    if first_rounds(c):
                        mark_8(DSA_BLOCKS[0])
                def minimum(i):
                    b, _ = STEPS[i]
                    _, logits, probs, _, _, at = step_bufs(i)
                    if b in DSA_BLOCKS:
                        dve.wait_ge(bias_made, DSA_BLOCKS.index(b) + 1)
                    dve.wait_ge(logits_done, i + 1)
                    if i >= 4:
                        dve.wait_ge(probs_turned, i - 3)
                    nc.vector.tensor_tensor_reduce(
                        out=probs, in0=logits, in1=select_bias[:, to_query[b]:to_query[b + 1]],
                        scale=-HEAD_DIM ** -0.5, scalar=-UNSELECTED, op0=ALU.add, op1=ALU.min,
                        accum_out=minus_max[:, at]).then_inc(max_done, 1)

                latent_parts(1)
                first_block, middle_block, last_block = DSA_BLOCKS
                for _ in range(TOP_K // 8 - sum(first_rounds(c) for c in range(len(DOTS)))):
                    find_8(first_block)
                    mark_8(first_block)
                choice_to_bias(first_block)
                dve.wait_ge(causal_done, 5)
                for n in range(TOP_K // 8):
                    find_8(middle_block)
                    if n < EARLY_ROUNDS:
                        find_8(last_block)
                    mark_8(middle_block)
                    if n < EARLY_ROUNDS:
                        mark_8(last_block)
                choice_to_bias(middle_block)
                minimum(0)
                minimum(1)

                def normalise(i):
                    _, _, probs, _, _, at = step_bufs(i)
                    dve.wait_ge(exp_done, i + 1)
                    inverted = count_step(nc.vector.reciprocal(row_inv[:, at], row_sum[:, at]))
                    if i - 1 in ROUND_STEPS:
                        mark_8(last_block)
                    dve.wait_ge(vector_step, inverted)
                    nc.vector.tensor_scalar(probs, probs, row_inv[:, at], None, ALU.mult)\
                        .then_inc(probs_done, 1)

                def result_lo(q):
                    dve.wait_ge(o_hi_made, q + 1)
                    nc.vector.tensor_tensor(four_heads(o_lo, q),
                                            results_bank(q)[:, :].rearrange("p (h t) -> p h t", h=4),
                                            four_heads(o_hi, q).bitcast(FP32), ALU.subtract)\
                        .then_inc(o_lo_made, 1)

                for i in range(len(STEPS)):
                    normalise(i)
                    if i + 2 < len(STEPS):
                        minimum(i + 2)
                    if i in ROUND_STEPS:
                        find_8(last_block)
                    elif i == ROUND_STEPS[-1] + 1:
                        choice_to_bias(last_block)
                    if i % 4 == 2 and i > 4:
                        result_lo(i // 4 - 1)
                result_lo(len(STEPS) // 4 - 1)
                dve.wait_ge(w_lo_made, u0 + POOL_SPLITS[1])
                for d in range(CHUNKS):
                    u = u0 + DSA_UNITS - DSA_OUT_UNITS + d // 2
                    if d % 2 == 0:
                        dve.wait_ge(half_done, 2 * RET_HEADS + d // 2 + 1)
                    else:
                        dve.wait_ge(unit_done, u + 1)
                    update(s, d, d % 2, 1.0)
                    if d % 2 == 1:
                        split_unit(u + 2)
                    stream_lo(s + 1, d)
        final = len(SUBLAYERS)
        mean_square(("norm", final), D_MODEL)
        dve.wait_ge(r_col_done, stat_count(("norm", final)))
        for b in range(BLOCKS):
            nc.vector.tensor_scalar(tile(diagonal, b), identity[:, :], r_col[:, b:b + 1], None,
                                    ALU.mult).then_inc(final_diagonal_done, 1)
        dve.wait_ge(broadcast_done, broadcast_count(("norm", final)))
        for k in range(CHUNKS):
            nc.vector.scalar_tensor_tensor(cols(x_res, k), cols(x_res, k), gain(final, k),
                                           bank[STAT_BANK][:, :], ALU.mult, ALU.mult)\
                .then_inc(y_done, 1)

    @block.tensor
    def _(pe):
        mm = nc.tensor.matmul

        def product(to, slot, at, hi, lo, start, stop, width=P):
            mm(to, w_hi[slot][:, at:at + width], hi, start=start, stop=False)
            mm(to, w_hi[slot][:, at:at + width], lo, start=False, stop=False)
            return mm(to, w_lo[slot][:, at:at + width], hi, start=False, stop=stop)

        def product_by_token(to, hi, lo, slot, at, width, start, stop):
            mm(to, hi, w_hi[slot][:, at:at + width], start=start, stop=False)
            mm(to, hi, w_lo[slot][:, at:at + width], start=False, stop=False)
            return mm(to, lo, w_hi[slot][:, at:at + width], start=False, stop=stop)

        def from_stream(to, slot, first_tile, ready=None):
            for k in range(CHUNKS):
                if ready is not None:
                    pe.wait_ge(xn_lo_made, ready + k + 1)
                done = product(to[:, :], slot, (first_tile + k) * P, cols(xn_hi, k), cols(xn_lo, k),
                               k == 0, k == CHUNKS - 1)
            return done

        def sum_over_features(which):
            pe.wait_ge(squares_done, squares_before(which) + square_ops(which))
            for b in range(BLOCKS):
                done = mm(bank[STAT_BANK][:, b:b + 1], tile(square_sum, b), ones[:, :1], start=True,
                          stop=True)
            done.then_inc(stat_done, 1)

        def broadcast(which):
            pe.wait_ge(diagonal_done, broadcast_count(which))
            mm(bank[STAT_BANK][:, :], ones[:, :], diagonal[:, :], start=True, stop=True)\
                .then_inc(broadcast_done, 1)

        pe.wait_ge(consts_made, 4)
        for s, kind in enumerate(SUBLAYERS):
            u0, tile0 = FIRST_UNIT[s], FIRST_TILE[s]
            norm = ("norm", s)
            if kind == "ffn":
                def in_pair(first, pair):
                    for n in range(2):
                        step = 2 * first + n
                        late = int(s == 0)
                        if step == 0 and s == 0:
                            pe.wait_ge(gate0_lo_made, 1)
                        else:
                            pe.wait_ge(w_lo_made, u0 + step + 1 + 2 * pair)
                        if step >= 2:
                            pe.wait_ge(temp_filled, tile0 + step - 1 + 2 * pair)
                        from_stream(bank[2 * n], n, 0, CHUNKS * s if step == 0 else None)
                        if step == 0 and not late:
                            sum_over_features(norm)
                        if step == 1 and late:
                            broadcast(norm)
                        if step == 0 and s == 0:
                            pe.wait_ge(w_lo_made, 1)
                        from_stream(bank[2 * n + 1], n, CHUNKS).then_inc(unit_done, 1)
                        if step == 0:
                            (sum_over_features if late else broadcast)(norm)

                in_pair(0, 0)
                with pe.Fori(0, FFN_IN_UNITS // 2 - 1) as i:
                    in_pair(1, i)

                def out_tile(d, n, pair):
                    if d >= 2:
                        pe.wait_ge(x_updated, CHUNKS * s + d - 1 + pair)
                    for half in range(2):
                        pe.wait_ge(w_lo_made, u0 + FFN_IN_UNITS + 2 * d + half + 1 + 2 * pair)
                        for kk in range(HALF_TILES):
                            k = HALF_TILES * half + kk
                            if d == 0:
                                pe.wait_ge(gated_lo_made, tile0 + k + 1)
                            done = product(bank[4 + n][:, :], half, kk * P, cols(gated_hi, k),
                                           cols(gated_lo, k), k == 0, k == FF_TILES - 1)
                        done.then_inc(unit_done, 1)

                for n in range(2):
                    out_tile(n, n, 0)
                with pe.Fori(0, CHUNKS // 2 - 1) as i:
                    for n in range(2):
                        out_tile(2 + n, n, 2 * i)
            elif kind == "ret":
                for h in range(RET_HEADS):
                    u = u0 + RET_HEAD_UNITS * h
                    for n in range(2):
                        pe.wait_ge(w_lo_made, u + 1 + n)
                        if n == 0 and h > 0:
                            pe.wait_ge(temp_filled, tile0 + V_TILES * h - 2)
                        if n == 1 and h > 0:
                            pe.wait_ge(temp_filled, tile0 + V_TILES * h)
                        from_stream(bank[4 + 2 * n], n, 0, CHUNKS * s if h == 0 and n == 0 else None)
                        if h == 0 and n == 0:
                            sum_over_features(norm)
                        if h == 0 and n == 1:
                            pe.wait_ge(r_ready, broadcast_count(norm))
                        from_stream(bank[5 + 2 * n], n, CHUNKS).then_inc(unit_done, 1)
                        if h == 0 and n == 0:
                            broadcast(norm)
                    if h > 0:
                        pe.wait_ge(gated_done, tile0 + V_TILES * h)
                    for half in range(2):
                        pe.wait_ge(w_lo_made, u + 3 + half)
                        for kk in range(CHUNKS // 2):
                            k = CHUNKS // 2 * half + kk
                            for b in range(BLOCKS):
                                done = product_by_token(
                                    bank[b][:, :], tile(xn_hi, k * BLOCKS + b),
                                    tile(xn_lo, k * BLOCKS + b), half, kk * RET_DV, RET_DV,
                                    k == 0, k == CHUNKS - 1)
                        done.then_inc(unit_done, 1)
                    pe.wait_ge(qk_rotated, 2 * h + 2)
                    for j in range(BLOCKS):
                        for n in range(2):
                            done = mm(bank[4 + j][:, :SEQ - P * j], tile(k_rot, n * BLOCKS + j),
                                      q_rot[:, n * SEQ + P * j:(n + 1) * SEQ], start=n == 0,
                                      stop=n == 1)
                        done.then_inc(scores_done, 1)
                    pe.wait_ge(v_scaled, BLOCKS * (h + 1))
                    for e in range(V_TILES):
                        for j in range(BLOCKS):
                            if e == 0:
                                pe.wait_ge(scores_decayed, BLOCKS * h + j + 1)
                            done = mm(bank[e][:, P * j:], tile(v_tok, j * V_TILES + e),
                                      scores[:, from_key[j]:from_key[j + 1]], start=j == 0,
                                      stop=j == BLOCKS - 1)
                        done.then_inc(ret_out_done, 1)
                    for e in range(V_TILES):
                        if e % 2 == 0:
                            pe.wait_ge(w_lo_made, u + 5 + e // 2)
                        if e == 3:
                            pe.wait_ge(r_ready, broadcast_count(("head", h)))
                        from_stream(bank[4 + e], e // 2, e % 2 * CHUNKS)\
                            .then_inc(unit_done if e % 2 else half_done, 1)
                        if e == 0:
                            sum_over_features(("head", h))
                        if e == 1:
                            broadcast(("head", h))

                def out_tile(d, n, pair):
                    if d >= 2:
                        pe.wait_ge(x_updated, CHUNKS * s + d - 1 + pair)
                    pe.wait_ge(w_lo_made, u0 + RET_IN_UNITS + d + 1 + pair)
                    for k in range(RET_TILES):
                        if d == 0:
                            pe.wait_ge(gated_lo_made, tile0 + k + 1)
                        done = product(bank[4 + n][:, :], n, k * P, cols(ret_hi, k), cols(ret_lo, k),
                                       k == 0, k == RET_TILES - 1)
                    done.then_inc(unit_done, 1)

                for n in range(2):
                    out_tile(n, n, 0)
                with pe.Fori(0, CHUNKS // 2 - 1) as i:
                    for n in range(2):
                        out_tile(2 + n, n, 2 * i)
            else:
                def latent_products(slot, part, k, at):
                    for b in range(BLOCKS):
                        done = product_by_token(
                            bank[b][:, part * RANK:(part + 1) * RANK], tile(xn_hi, k * BLOCKS + b),
                            tile(xn_lo, k * BLOCKS + b), slot, at, RANK, k == 0, k == CHUNKS - 1)
                    return done

                def turn_latents(part):
                    pe.wait_ge(latents_scaled, (part + 1) * BLOCKS)
                    for n in range(2):
                        for b in range(BLOCKS):
                            done = nc.tensor.transpose(tile(latent_bank(2 * part + n), b),
                                                       tile(latents, (part * BLOCKS + b) * 2 + n),
                                                       identity[:, :])
                        done.then_inc(latents_turned, 1)

                pe.wait_ge(w_lo_made, u0 + 1)
                for k in range(CHUNKS):
                    pe.wait_ge(xn_lo_made, CHUNKS * s + k + 1)
                    done = latent_products(0, 0, k, k * RANK)
                    if k == CHUNKS - 1:
                        done.then_inc(unit_done, 1)
                    if k == CHUNKS // 2 + 1:
                        sum_over_features(norm)
                pe.wait_ge(w_lo_made, u0 + 2)
                for k in range(CHUNKS):
                    done = product(bank[5][:IDX_COLS, :], 1, k * IDX_COLS, cols(xn_hi, k),
                                   cols(xn_lo, k), k == 0, k == CHUNKS - 1, IDX_COLS)
                done.then_inc(unit_done, 1)
                pe.wait_ge(latents_copied, BLOCKS)
                for half in range(2):
                    pe.wait_ge(w_lo_made, u0 + 3 + half)
                    for kk in range(CHUNKS // 2):
                        done = latent_products(half, 1, CHUNKS // 2 * half + kk, kk * RANK)
                        if (half, kk) == (0, 1):
                            pe.wait_ge(idx_copied, 1)
                            for b in range(BLOCKS):
                                turned = nc.tensor.transpose(
                                    bank[4][:, b * IDX_COLS:(b + 1) * IDX_COLS],
                                    tile(r_norm, b)[:IDX_COLS, :], identity[:IDX_COLS, :IDX_COLS])
                            turned.then_inc(idx_turned, 1)
                        if (half, kk) == (1, 2):
                            turn_latents(0)
                    done.then_inc(unit_done, 1)
                pe.wait_ge(k_scaled, 2 * BLOCKS)
                for b in range(BLOCKS):
                    done = nc.tensor.transpose(tile(bank[7], b), tile(k_twice, b), identity[:, :])
                done.then_inc(k_turned, 1)
                pe.wait_ge(latent_lo_made, 2)
                pe.wait_ge(w_lo_made, u0 + 5)
                for m in range(Q_IDX_TILES):
                    if m == Q_IDX_TILES - 1:
                        pe.wait_ge(k_idx_made, 1)
                    for n in range(2):
                        done = product(bank[DOT_BANKS[m]][:, :], 0, (n * Q_IDX_TILES + m) * P,
                                       latent_hi[n][:, :], latent_lo[n][:, :], n == 0, n == 1)
                    done.then_inc(q_idx_done if m < Q_IDX_TILES - 1 else unit_done, 1)
                for c, (b, hh) in enumerate(DOTS):
                    keys, at = P * (b + 1), IDX_DIM * (hh % 2)
                    if c < 4:
                        pe.wait_ge(q_idx_copied, Q_IDX_TILES)
                    else:
                        pe.wait_ge(relu_done, c - 3)
                    mm(bank[DOT_BANKS[c % 4]][:, :keys],
                       q_idx[at:at + IDX_DIM, hh // 2 * SEQ + b * P:hh // 2 * SEQ + (b + 1) * P],
                       k_idx[at:at + IDX_DIM, :keys], start=True, stop=True).then_inc(dots_done, 1)
                pe.wait_ge(latents_copied, 2 * BLOCKS)
                turn_latents(1)
                def logits(i):
                    b, h = STEPS[i]
                    if i < 3:
                        pe.wait_ge(proj_copied, FIRST_COPIED + i)
                    else:
                        pe.wait_ge(max_done, i - 2)
                    mm(step_bufs(i)[1], tile(q_heads, h * BLOCKS + b),
                       k_heads[:, h * SEQ:h * SEQ + P * (b + 1)], start=True, stop=True)\
                        .then_inc(logits_done, 1)

                for j in range(3 * 8):
                    slot = (u0 + 5 + j // 8) % 2
                    if j % 8 == 0:
                        pe.wait_ge(w_lo_made, u0 + 6 + j // 8)
                    if j == 2:
                        pe.wait_ge(relu_done, len(DOTS))
                    if j == 8:
                        pe.wait_ge(latent_lo_made, 4)
                    if j >= 4:
                        pe.wait_ge(proj_copied, j - 3)
                    if j in FIRST_LOGITS:
                        logits(FIRST_LOGITS.index(j))
                    to = bank[PROJ_BANKS[j % 4]][:, :]
                    for n in range(2):
                        if j < 16:
                            lat = 2 * (j // 8) + n
                            done = product(to, slot, (j % 8 * 2 + n) * P, latent_hi[lat][:, :],
                                           latent_lo[lat][:, :], n == 0, n == 1)
                        else:
                            b, half = (j - 16) // 2, j % 2
                            done = product_by_token(to, tile(latent_hi[2 + n], b),
                                                    tile(latent_lo[2 + n], b), slot,
                                                    n * D_MODEL + half * SEQ, SEQ, n == 0, n == 1)
                    done.then_inc(unit_done if j % 8 == 7 else proj_done, 1)

                def turn_probs(i):
                    b, _ = STEPS[i]
                    _, _, probs, turned, _, _ = step_bufs(i)
                    pe.wait_ge(probs_done, i + 1)
                    if i >= 2:
                        pe.wait_ge(probs_t_copied, i - 1)
                    for j in range(b + 1):
                        done = nc.tensor.transpose(tile(turned, j), tile(probs, j), identity[:, :])
                    done.then_inc(probs_turned, 1)

                def results(i):
                    b, h = STEPS[i]
                    pe.wait_ge(probs_t_copied, i + 1)
                    if i % 4 == 0 and i >= 12:
                        pe.wait_ge(o_lo_made, i // 4 - 2)
                    for j in range(b + 1):
                        done = mm(tile(results_bank(i // 4), h % 4), tile(v_heads, j * HEADS + h),
                                  tile(step_bufs(i)[4], j), start=j == 0, stop=j == b)
                    done.then_inc(o_done, 1)

                logits(2)
                pe.wait_ge(proj_copied, 3 * 8)
                for i in range(len(STEPS)):
                    turn_probs(i)
                    if i + 3 < len(STEPS):
                        logits(i + 3)
                    if i >= 1:
                        results(i - 1)
                results(len(STEPS) - 1)
                for d in range(CHUNKS):
                    u = u0 + DSA_UNITS - DSA_OUT_UNITS + d // 2
                    if d % 2 == 0:
                        pe.wait_ge(w_lo_made, u + 1)
                    if d >= 2:
                        pe.wait_ge(x_updated, CHUNKS * s + d - 1)
                    for k in range(HEADS):
                        if d == 0:
                            pe.wait_ge(o_lo_made, len(STEPS) // 4 - 1 + k // 4)
                        done = product(bank[4 + d % 2][:, :], u % 2, (d % 2 * HEADS + k) * P,
                                       cols(o_hi, k), cols(o_lo, k), k == 0, k == HEADS - 1)
                    done.then_inc(unit_done if d % 2 else half_done, 1)
        final = ("norm", len(SUBLAYERS))
        pe.wait_ge(squares_done, squares_before(final) + square_ops(final))
        pe.wait_ge(last_squared, 1)
        for b in range(BLOCKS):
            mm(bank[STAT_BANK][:, b:b + 1], tile(square_sum, b), ones[:, :1], start=True, stop=False)
            done = mm(bank[STAT_BANK][:, b:b + 1], tile(temp, b), ones[:, :1], start=False, stop=True)
        done.then_inc(stat_done, 1)
        for b in range(BLOCKS):
            pe.wait_ge(final_diagonal_done, b + 1)
            done = mm(tile(bank[STAT_BANK], b), ones[:, :], tile(diagonal, b), start=True, stop=True)
        done.then_inc(broadcast_done, 1)



def rotary_table():
    pairs = RET_DK // 2
    freq = np.float32(1.0) / np.float32(ROT_BASE) ** np.linspace(0.0, 1.0, pairs, dtype=np.float32)
    angle = (np.arange(SEQ, dtype=np.float32)[None, :] * freq.astype(np.float32)[:, None]).astype(np.float32)
    return np.stack([np.cos(angle), np.sin(angle)]).astype(np.float32)


def decay_table():
    log_gamma = np.log(1.0 - 2.0 ** (-5.0 - np.arange(RET_HEADS)))
    ahead = np.arange(SEQ)[None, :] - np.arange(P)[:, None]
    table = np.exp(np.maximum(ahead, 0)[None] * log_gamma[:, None, None]) * (ahead >= 0)[None]
    return (table * RET_DK ** -0.5).astype(np.float32)


def stationary(w):
    rows, columns = w.shape
    return w.reshape(rows // P, P, columns // P, P).transpose(2, 1, 0, 3)


def laid_out(a):
    f32 = {k: np.asarray(v) for k, v in a.items()}
    by_partition = lambda v: v.reshape(-1, P).T

    ffn_in, ffn_out = [], []
    for layer in range(f32["w_ffn1_in"].shape[0]):
        for name in ("w_ffn1", "w_ffn2"):
            t = stationary(f32[name + "_in"][layer])
            ffn_in.append(np.stack([t[:FF_TILES], t[FF_TILES:]], axis=2).reshape(FF_TILES, P, UNIT))
            t = stationary(f32[name + "_out"][layer])
            t = t.reshape(CHUNKS, P, 2, HALF_TILES, P).transpose(0, 2, 1, 3, 4)
            ffn_out.append(t.reshape(FFN_OUT_UNITS, P, OUT_UNIT))

    w = f32["ret_w_in"][0]
    qk, vg = RET_HEADS * RET_DK, RET_HEADS * RET_DV
    ret_in = []
    for h in range(RET_HEADS):
        for at in (0, qk):
            part = w[:, at + h * RET_DK:at + (h + 1) * RET_DK]
            pairs = part.reshape(D_MODEL, RET_DK // 2, 2).transpose(0, 2, 1).reshape(D_MODEL, RET_DK)
            ret_in.append(stationary(pairs).transpose(1, 0, 2, 3).reshape(P, UNIT))
        v = w[:, 2 * qk + h * RET_DV:2 * qk + (h + 1) * RET_DV].reshape(2, CHUNKS // 2, P, RET_DV)
        ret_in += list(v.transpose(0, 2, 1, 3).reshape(2, P, UNIT))
        g = stationary(w[:, 2 * qk + vg + h * RET_DV:2 * qk + vg + (h + 1) * RET_DV])
        ret_in += [g[2 * n:2 * n + 2].transpose(1, 0, 2, 3).reshape(P, UNIT) for n in range(2)]
    ret_out = stationary(f32["ret_w_out"][0]).reshape(CHUNKS, P, UNIT)

    w = f32["dsa_w_in"][0]
    dsa = [w[:, n * RANK:(n + 1) * RANK].reshape(CHUNKS, P, RANK).transpose(1, 0, 2).reshape(P, UNIT)
           for n in range(2)]
    for name in ("dsa_w_uq", "dsa_w_uk"):
        dsa.append(stationary(f32[name][0].reshape(RANK, D_MODEL)).transpose(1, 0, 2, 3).reshape(P, UNIT))
    dsa.append(f32["dsa_w_uv"][0].reshape(2, P, D_MODEL).transpose(1, 0, 2).reshape(P, UNIT))
    t = stationary(f32["dsa_w_out"][0])
    dsa += [t[2 * n:2 * n + 2].transpose(1, 0, 2, 3).reshape(P, UNIT) for n in range(DSA_OUT_UNITS)]
    idx = w[:, 2 * RANK:].reshape(CHUNKS, P, IDX_COLS).transpose(1, 0, 2).reshape(P, -1)
    q_idx = f32["dsa_w_qidx"][0].reshape(2, P, IDX_HEADS * IDX_DIM).transpose(1, 0, 2).reshape(P, -1)

    norms = []
    for layer in range(f32["norm_mix"].shape[0]):
        norms += [by_partition(f32[n][layer]) for n in ("norm_ffn1", "norm_mix", "norm_ffn2")]
    norms += [by_partition(f32["final_norm"])]
    norms += [by_partition(f32[n][0]) for n in ("dsa_q_norm", "dsa_kv_norm")]
    norms += [by_partition(np.tile(f32[n][0], 2)) for n in ("dsa_kidx_g", "dsa_kidx_b")]

    x = f32["x"][0]
    return {
        "x_in": x.T.reshape(CHUNKS, P, SEQ).transpose(1, 0, 2).reshape(P, CHUNKS * SEQ),
        "w_ffn_in": np.concatenate(ffn_in),
        "w_ffn_out": np.concatenate(ffn_out),
        "w_ret_in": np.stack(ret_in),
        "w_ret_out": ret_out,
        "w_dsa": np.stack(dsa),
        "w_dsa_idx": np.concatenate([idx, q_idx], axis=1),
        "gains_in": np.concatenate(norms, axis=1),
        "rotary_in": rotary_table(),
        "decay_in": decay_table(),
    }


def kernel(**inputs):
    import concourse.bacc as bacc
    from concourse.bass_utils import run_bass_kernel_spmd

    nc = bacc.Bacc("TRN2", target_bir_lowering=False, num_devices=1)
    arrays = {k: np.ascontiguousarray(v) for k, v in laid_out(inputs).items()}
    args = {k: nc.dram_tensor(k, v.shape, mybir.dt.from_np(v.dtype), kind="ExternalInput").ap()
            for k, v in arrays.items()}
    out = nc.dram_tensor("out", (P, CHUNKS, SEQ), FP32, kind="ExternalOutput").ap()
    hybrid_trunk_kernel(nc, *args.values(), out)
    result = run_bass_kernel_spmd(nc, [arrays], core_ids=[0]).results[0]["out"]
    return np.ascontiguousarray(result.transpose(2, 1, 0).reshape(1, SEQ, D_MODEL))
```
